# Optimizing a Trainium2 kernel written in Bass

```python
import math
import jax, jax.numpy as jnp
from jax import lax
import numpy as np

D_MODEL = 1024
BATCH = 1
SEQ = 512
DEPTH = 2

HEAD_DIM = 64
ROPE_THETA = 10000.0
NORM_EPS = 1e-6
BLOCK = 128
NEG_INF = -1e30
A_Q_HEADS = 8
A_KV_HEADS = 2
A_HALF_WINDOW = 128
B_GROUPS = ((128, 1), (512, 4), (2048, 16))
B_HEADS_PER_GROUP = 4
MOE_GROUPS = 4
EXPERTS_PER_GROUP = 8
N_EXPERTS = MOE_GROUPS * EXPERTS_PER_GROUP
EXPERT_TOP_K = 2
D_EXPERT = 256
MOE_CHUNK = 1024

A_Q_DIM = A_Q_HEADS * HEAD_DIM
A_KV_DIM = A_KV_HEADS * HEAD_DIM
B_DIM = B_HEADS_PER_GROUP * HEAD_DIM
IN_SPLITS = [A_Q_DIM, A_KV_DIM, A_KV_DIM] + [B_DIM] * (3 * len(B_GROUPS)) + [D_MODEL, D_MODEL]
D_IN = sum(IN_SPLITS)
IN_OFFSETS = [int(v) for v in np.cumsum(IN_SPLITS)[:-1]]

kernel_name = 'hybrid_gqa_dilated_hmoe_encoder'

def rms_norm(x, g):
    xf = x.astype(jnp.float32)
    y = xf * lax.rsqrt(jnp.mean(xf * xf, axis=-1, keepdims=True) + NORM_EPS)
    return (y * g.astype(jnp.float32)).astype(x.dtype)

def rotary_tables(seq_len):
    inv = 1.0 / (ROPE_THETA ** (jnp.arange(0, HEAD_DIM, 2, dtype=jnp.float32) / HEAD_DIM))
    ang = jnp.arange(seq_len, dtype=jnp.float32)[:, None] * inv[None, :]
    return jnp.cos(ang), jnp.sin(ang)

def apply_rope(t, cos, sin):
    half = t.shape[-1] // 2
    t1 = t[..., :half].astype(jnp.float32)
    t2 = t[..., half:].astype(jnp.float32)
    c = cos[None, :, None, :]
    s = sin[None, :, None, :]
    return jnp.concatenate([t1 * c - t2 * s, t2 * c + t1 * s], axis=-1).astype(t.dtype)

def banded_attention(q, k, v, half_window, sink):
    B, L, Hq, dh = q.shape
    Hkv = k.shape[2]
    G = Hq // Hkv
    blk = math.gcd(L, BLOCK)
    nb = L // blk
    kw = blk + 2 * half_window
    pad = ((0, 0), (half_window, half_window), (0, 0), (0, 0))
    kp = jnp.pad(k, pad)
    vp = jnp.pad(v, pad)
    key_idx = jnp.arange(nb)[:, None] * blk + jnp.arange(kw)[None, :]
    kb = kp[:, key_idx]
    vb = vp[:, key_idx]
    qb = q.reshape(B, nb, blk, Hkv, G, dh)
    s = jnp.einsum('bnqhgd,bnkhd->bnhgqk', qb, kb).astype(jnp.float32) * (dh ** -0.5)
    qpos = jnp.arange(nb)[:, None] * blk + jnp.arange(blk)[None, :]
    kpos = key_idx - half_window
    rel = kpos[:, None, :] - qpos[:, :, None]
    valid = (jnp.abs(rel) <= half_window) & (kpos >= 0)[:, None, :] & (kpos < L)[:, None, :]
    s = jnp.where(valid[None, :, None, None], s, NEG_INF)
    m = jnp.max(s, axis=-1)
    if sink is not None:
        sk = sink.astype(jnp.float32).reshape(Hkv, G)[None, None, :, :, None]
        m = jnp.maximum(m, sk)
        denom = jnp.sum(jnp.exp(s - m[..., None]), axis=-1) + jnp.exp(sk - m)
    else:
        denom = jnp.sum(jnp.exp(s - m[..., None]), axis=-1)
    lse = m + jnp.log(denom)
    p = jnp.exp(s - lse[..., None]).astype(v.dtype)
    out = jnp.einsum('bnhgqk,bnkhd->bnqhgd', p, vb).reshape(B, L, Hq, dh)
    lse = lse.transpose(0, 1, 4, 2, 3).reshape(B, L, Hq)
    return out, lse

def dilated_attention(q, k, v, window, dilation):
    B, S, H, dh = q.shape
    L = S // dilation

    def to_sub(t):
        return t.reshape(B, L, dilation, H, dh).transpose(0, 2, 1, 3, 4).reshape(B * dilation, L, H, dh)

    o, lse = banded_attention(to_sub(q), to_sub(k), to_sub(v), (window // 2) // dilation, None)
    o = o.reshape(B, dilation, L, H, dh).transpose(0, 2, 1, 3, 4).reshape(B, S, H, dh)
    lse = lse.reshape(B, dilation, L, H).transpose(0, 2, 1, 3).reshape(B, S, H)
    return o, lse

def hier_moe(h, w_rg, b_rg, w_re, b_re, w_g, w_u, w_d):
    B, S, D = h.shape
    t = h.reshape(B * S, D)
    T = t.shape[0]
    glog = (t @ w_rg).astype(jnp.float32) + b_rg.astype(jnp.float32)
    gprob = jax.nn.softmax(glog, axis=-1)
    gidx = jnp.argmax(glog, axis=-1)
    gw = jnp.take_along_axis(gprob, gidx[:, None], axis=1)
    elog = ((t @ w_re).astype(jnp.float32) + b_re.astype(jnp.float32)).reshape(T, MOE_GROUPS, EXPERTS_PER_GROUP)
    elog = jnp.take_along_axis(elog, gidx[:, None, None], axis=1)[:, 0]
    top_v, top_i = lax.top_k(elog, EXPERT_TOP_K)
    top_w = jax.nn.softmax(top_v, axis=-1) * gw
    eid = gidx[:, None] * EXPERTS_PER_GROUP + top_i
    combine = jnp.sum(jax.nn.one_hot(eid, N_EXPERTS, dtype=jnp.float32) * top_w[..., None], axis=1)
    C = math.gcd(T, MOE_CHUNK)

    def run(args):
        tc, cc = args
        a = jnp.einsum('cd,edf->cef', tc, w_g)
        u = jnp.einsum('cd,edf->cef', tc, w_u)
        z = jax.nn.silu(a) * u * cc[..., None].astype(tc.dtype)
        return jnp.einsum('cef,efd->cd', z, w_d)

    y = lax.map(run, (t.reshape(T // C, C, D), combine.reshape(T // C, C, N_EXPERTS)))
    return y.reshape(B, S, D)

def setup_inputs(seed: int = 0) -> dict:
    key = jax.random.key(seed)
    ks = jax.random.split(key, 16)
    f32 = jnp.float32
    nrm = lambda k, shape, scale: jax.random.normal(k, shape, f32) * scale
    return {
        'x': jax.random.normal(ks[0], (BATCH, SEQ, D_MODEL), f32),
        'attn_norm_g': 1.0 + nrm(ks[1], (DEPTH, D_MODEL), 0.01),
        'w_in': nrm(ks[2], (DEPTH, D_MODEL, D_IN), D_MODEL ** -0.5),
        'a_sink': nrm(ks[3], (DEPTH, A_Q_HEADS), 0.5),
        'w_branch_a': nrm(ks[4], (DEPTH, A_Q_DIM, D_MODEL), A_Q_DIM ** -0.5),
        'w_branch_b': nrm(ks[5], (DEPTH, B_DIM, D_MODEL), B_DIM ** -0.5),
        'w_out': nrm(ks[6], (DEPTH, D_MODEL, D_MODEL), D_MODEL ** -0.5),
        'ffn_norm_g': 1.0 + nrm(ks[7], (DEPTH, D_MODEL), 0.01),
        'w_router_group': nrm(ks[8], (DEPTH, D_MODEL, MOE_GROUPS), D_MODEL ** -0.5),
        'b_router_group': nrm(ks[9], (DEPTH, MOE_GROUPS), 0.01),
        'w_router_expert': nrm(ks[10], (DEPTH, D_MODEL, N_EXPERTS), D_MODEL ** -0.5),
        'b_router_expert': nrm(ks[11], (DEPTH, N_EXPERTS), 0.01),
        'w_exp_gate': nrm(ks[12], (DEPTH, N_EXPERTS, D_MODEL, D_EXPERT), D_MODEL ** -0.5),
        'w_exp_up': nrm(ks[13], (DEPTH, N_EXPERTS, D_MODEL, D_EXPERT), D_MODEL ** -0.5),
        'w_exp_down': nrm(ks[14], (DEPTH, N_EXPERTS, D_EXPERT, D_MODEL), D_EXPERT ** -0.5),
        'final_norm_g': 1.0 + nrm(ks[15], (D_MODEL,), 0.01),
    }

def reference(x, attn_norm_g, w_in, a_sink, w_branch_a, w_branch_b, w_out, ffn_norm_g,
              w_router_group, b_router_group, w_router_expert, b_router_expert,
              w_exp_gate, w_exp_up, w_exp_down, final_norm_g):
    B, S, D = x.shape
    cos, sin = rotary_tables(S)
    for l in range(DEPTH):
        h = rms_norm(x, attn_norm_g[l])
        proj = jnp.einsum('bsd,de->bse', h, w_in[l])
        parts = jnp.split(proj, IN_OFFSETS, axis=-1)
        qa = apply_rope(parts[0].reshape(B, S, A_Q_HEADS, HEAD_DIM), cos, sin)
        ka = apply_rope(parts[1].reshape(B, S, A_KV_HEADS, HEAD_DIM), cos, sin)
        va = parts[2].reshape(B, S, A_KV_HEADS, HEAD_DIM)
        ya, _ = banded_attention(qa, ka, va, A_HALF_WINDOW, a_sink[l])
        ya = jnp.einsum('bse,ed->bsd', ya.reshape(B, S, A_Q_DIM), w_branch_a[l])
        outs, lses = [], []
        for gi, (win, dil) in enumerate(B_GROUPS):
            qg = apply_rope(parts[3 + 3 * gi].reshape(B, S, B_HEADS_PER_GROUP, HEAD_DIM), cos, sin)
            kg = apply_rope(parts[4 + 3 * gi].reshape(B, S, B_HEADS_PER_GROUP, HEAD_DIM), cos, sin)
            vg = parts[5 + 3 * gi].reshape(B, S, B_HEADS_PER_GROUP, HEAD_DIM)
            o, lse = dilated_attention(qg, kg, vg, win, dil)
            outs.append(o)
            lses.append(lse)
        wg = jax.nn.softmax(jnp.stack(lses, axis=0), axis=0)
        yb = jnp.sum(wg[..., None].astype(x.dtype) * jnp.stack(outs, axis=0), axis=0)
        yb = jnp.einsum('bse,ed->bsd', yb.reshape(B, S, B_DIM), w_branch_b[l])
        merged = jax.nn.sigmoid(parts[-2]) * ya + jax.nn.sigmoid(parts[-1]) * yb
        x = x + jnp.einsum('bsd,de->bse', merged, w_out[l])
        x = x + hier_moe(rms_norm(x, ffn_norm_g[l]), w_router_group[l], b_router_group[l],
                         w_router_expert[l], b_router_expert[l],
                         w_exp_gate[l], w_exp_up[l], w_exp_down[l])
    return rms_norm(x, final_norm_g)


_drawn_inputs = setup_inputs


def setup_inputs(seed=0):
    import zlib

    import numpy as np

    out = dict(_drawn_inputs(seed))
    spreads = {}
    factors = {'attn_norm_g': 3.298,
     'a_sink': 64.0,
     'b_router_expert': 2.694,
     'final_norm_g': 32.805,
     'b_router_group': 6.032}
    for name, (base, spread) in spreads.items():
        noise = np.random.default_rng([zlib.crc32(name.encode()), seed]).standard_normal(out[name].shape)
        drawn = base * np.exp(spread * noise) if base else spread * noise
        out[name] = __import__('jax').numpy.asarray(drawn.astype(out[name].dtype))
    for name, factor in factors.items():
        out[name] = (out[name] * factor).astype(out[name].dtype)
    return out
```

```python
import math
from contextlib import ExitStack

import concourse.bass as bass
from concourse import mybir

FP32 = mybir.dt.float32
F32R = mybir.dt.float32r
BF16 = mybir.dt.bfloat16
I32 = mybir.dt.int32
U32 = mybir.dt.uint32
ALU = mybir.AluOpType
ACT = mybir.ActivationFunctionType
AX = mybir.AxisListType

P = 128
T = 512
TT = T // P
D = 1024
KD = D // P
DH = 64
EPS = 1e-6
SCALE = DH ** -0.5
NE = 32
NGRP = 4
EPG = NE // NGRP
FE = 256
CAP = 64
PAIRS = NE // 2
BIG = 4096.0
NEVER = 1000.0
NLOG = NGRP + NE
PARAMS = KD * NLOG + NLOG + KD + 8

V, R = "v", "rope"
BLOCK_A = [(V, 0), (R, 4), (R, 0), (R, 1), (R, 2), (R, 3)]
BLOCK_B = [(V, 0), (V, 1), (V, 2), (R, 0), (R, 1), (R, 2), (R, 3), (R, 4), (R, 5)]
BLOCKS = [BLOCK_A, BLOCK_B, BLOCK_B]
QKV = [(b, kind, idx) for b, blk in enumerate(BLOCKS) for kind, idx in blk]
NQ = len(QKV)
NGATE = 3 * KD
NOUT = 8
NT = NQ + NGATE + NOUT
ROPES = [sum(1 for q in QKV[:i] if q[1] == R) for i in range(NQ + 1)]
VS = [sum(1 for q in QKV[:i] if q[1] == V) for i in range(NQ + 1)]
BLOCK_AT = [0, len(BLOCK_A), len(BLOCK_A) + len(BLOCK_B)]
NSTEP_A, NSTEP_B = 16, 4
STEPS = NSTEP_A + 2 * NSTEP_B
C_COS, C_SIN, C_ID, C_TRI, C_ONE, C_IOTA = 0, 512, 1024, 1152, 1280, 1408
C_TOK = C_IOTA + CAP
C_THR = C_TOK + 8
C_END = C_THR + 8
MA, MB = 3 * P, T + 2 * P


def hybrid_encoder(nc, x_in, stream, gu_w, dn_w, params, g_rows, consts, masks, out):
    L = stream.shape[0]
    y_rows = nc.dram_tensor("y_rows", (2 * T, D), FP32, kind="Internal").ap()

    def at(name, offset, shape, dt):
        return nc.alloc_sbuf_tensor_at(name, [P, *shape], dt, offset=offset)

    def after(n):
        return -(-n // 32) * 32

    KB = 1024
    base = after(nc.sbuf_base)
    R_X, R_C, R_W, R_H, R_Q, R_S = (base + n * KB for n in (0, 16, 31, 79, 135, 183))
    x = at("x", R_X, [TT, D], FP32)
    cst = at("cst", R_C, [C_END], FP32)
    o = R_C + 4 * C_END
    mask_a = at("mask_a", o, [MA], BF16); o = after(o + 2 * MA)
    mask_b = at("mask_b", o, [TT, T], BF16); o = after(o + 2 * TT * T)
    mask_b12 = at("mask_b12", o, [2 * P], BF16); o = after(o + 4 * P)
    par = at("par", o, [PARAMS], FP32); o = after(o + 4 * PARAMS)
    wr = par[:, 0:KD * NLOG].rearrange("p (k n) -> p k n", n=NLOG)
    br = par[:, KD * NLOG:KD * NLOG + NLOG]
    g_col = par[:, KD * NLOG + NLOG:KD * NLOG + NLOG + KD]
    sink = par[:, KD * NLOG + NLOG + KD:PARAMS]
    nsink = at("nsink", o, [8], FP32); o = after(o + 32)
    small = at("small", o, [96], FP32); o = after(o + 4 * 96)
    assert o <= R_W, o
    gu = [at("gu0", R_W, [2, KD, 2 * FE], FP32), at("gu1", R_H, [2, KD, 2 * FE], FP32)]
    dn = [at("dn0", R_W + 32 * KB, [2, 2, D], FP32), at("dn1", R_H + 32 * KB, [2, 2, D], FP32)]
    h_hi = at("h_hi", R_H, [KD, T], F32R)
    h_lo = at("h_lo", R_H + 16 * KB, [KD, T], F32R)
    o_hi = at("o_hi", R_H + 32 * KB, [6, T], F32R)
    o_lo = at("o_lo", R_H + 44 * KB, [6, T], F32R)
    qk_a = at("qk_a", R_Q, [5, T], FP32)
    v_a = at("v_a", R_Q + 10 * KB, [TT, P], FP32)
    qk_b = at("qk_b", R_Q + 12 * KB, [6, T], FP32)
    v_b = at("v_b", R_Q + 24 * KB, [3, TT, P], FP32)
    vt = at("vt", R_Q + 30 * KB, [2, T], FP32)
    swp = at("swp", R_Q + 34 * KB, [2, T], FP32)
    rca = at("rca", R_Q + 38 * KB, [2, T], FP32)
    prob = at("prob", R_Q + 30 * KB, [2, 2, MB], FP32)
    pt = at("pt", R_Q + 42 * KB, [2, MB], FP32)
    m_hi = at("m_hi", R_Q, [KD, T], F32R)
    m_lo = at("m_lo", R_Q + 16 * KB, [KD, T], F32R)
    sg = at("sg", R_Q + 32 * KB, [2, 2, T], FP32)
    mab = at("mab", R_Q + 40 * KB, [2, 2, T], FP32)
    xn = at("xn", R_Q, [TT, D], FP32)
    h2_hi = at("h2_hi", R_Q, [TT, D], F32R)
    h2_lo = at("h2_lo", R_Q + 16 * KB, [TT, D], F32R)
    yb = at("yb", R_Q + 32 * KB, [2, D], FP32)
    xn2 = yb
    junk = at("junk", R_Q + 32 * KB, [TT, D], BF16)
    g_row = at("g_row", R_Q + 40 * KB, [D], FP32)
    sel = at("sel", R_Q + 40 * KB, [2, TT, P], F32R)
    z = at("z", R_Q + 44 * KB, [FE], FP32)
    zt = at("zt", R_Q + 45 * KB, [2, P], FP32)
    sil = at("sil", R_Q + 46 * KB, [FE], FP32)
    yld = at("yld", R_Q, [2, TT, D], FP32)
    raw = at("raw", R_S, [2, 1024], FP32)
    w_hi = [at(f"w_hi{i}", R_S + (8 + 8 * i) * KB, [1024], F32R) for i in range(2)]
    w_lo = [at(f"w_lo{i}", R_S + (12 + 8 * i) * KB, [1024], F32R) for i in range(2)]
    h2t = at("h2t", R_S + 8 * KB, [KD, T], FP32)
    xg = at("xg", R_S + 8 * KB, [D], FP32)
    xgt = at("xgt", R_S + 12 * KB, [KD, P], FP32)
    rt = at("rt", R_S + 16 * KB, [1900], FP32)
    mask_f32 = at("mask_f32", R_Q, [MA + TT * T + 2 * P], FP32)

    def c(a, n):
        return cst[:, a:a + n]

    ident = c(C_ID, P)

    _w = [0]

    def word(n, *shape):
        a = _w[0]
        _w[0] += n
        v = rt[:, a:a + n]
        if len(shape) == 2:
            v = v.rearrange("p (a b) -> p a b", b=shape[1])
        if len(shape) == 3:
            v = v.rearrange("p (a b c) -> p a b c", b=shape[1], c=shape[2])
        return v

    rankm = word(TT * NE, TT, NE)
    info = word(TT * 2 * NE, TT, 2, NE)
    logit = word(TT * NLOG, TT, NLOG)
    gl8 = word(TT * 8, TT, 8)
    top_g = word(TT * 8, TT, 8)
    idx_g = word(TT * 8, TT, 8)
    top_e = word(TT * 8, TT, 8)
    idx_e = word(TT * 8, TT, 8)
    idxf = word(TT * 3, TT, 3)
    oh_g = word(TT * NGRP, TT, NGRP)
    el8 = word(TT * 8, TT, 8)
    elm = word(TT * NE, TT, NGRP, EPG)
    oh1 = word(TT * NE, TT, NGRP, EPG)
    oh2 = word(TT * NE, TT, NGRP, EPG)
    oh8 = word(TT * 2 * EPG, TT, 2, EPG)
    asg = word(TT * NE, TT, NE)
    rtmp = word(TT * NE, TT, NE)
    ge = word(TT * NGRP, TT, NGRP)
    wts = word(TT * 8, TT, 8)
    assert _w[0] <= 1900, _w[0]
    more = small[:, 40:48]
    rounds_f = small[:, 48:50]
    rounds_i = at("rounds_i", R_C + 15 * KB - 64, [2 * 4], I32)
    idx_row = at("idx_row", R_C + 15 * KB - 32, [2], I32)
    wslot = small[:, 52:54]
    ss, ms, rs = small[:, 0:4], small[:, 4:8], small[:, 8:12]
    nt1, nt2 = small[:, 12:16], small[:, 16:20]
    nmx, den, es = small[:, 20:24], small[:, 24:28], small[:, 28:32]
    nm2 = small[:, 32:36]
    rsum = small[:, 36:40]
    cnt_s = small[:, 56:64]

    ctx = ExitStack()
    with ctx:
        bank = [ctx.enter_context(nc.psum_tensor(f"bank{i}", [P, T], FP32)) for i in range(8)]

        def sem(name):
            return ctx.enter_context(nc.semaphore(name))

        cst_ld, x_ld, par_ld, gr_ld = sem("cst_ld"), sem("x_ld"), sem("par_ld"), sem("gr_ld")
        x_ok, sn_ok = sem("x_ok"), sem("sn_ok")
        raw_ld = [sem("raw_ld0"), sem("raw_ld1")]
        hi_ok, lo_ok, w_used = sem("hi_ok"), sem("lo_ok"), sem("w_used")
        sq_ok, ms_ok, rt_ok, rs_ok, xn_ok, xt_ok = (sem(n) for n in ("sq_ok", "ms_ok", "rt_ok", "rs_ok", "xn_ok", "xt_ok"))
        hhi_ok, hlo_ok = sem("hhi_ok"), sem("hlo_ok")
        pj_act, pj_dve, rope_ok = (sem(n) for n in ("pj_act", "pj_dve", "rope_ok"))
        vt_ok, v_ok = sem("vt_ok"), sem("v_ok")
        sc_ok, mx_ok, dn1_ok, ex_ok, pr_ok, tr_ok = (sem(n) for n in ("sc_ok", "mx_ok", "dn1_ok", "ex_ok", "pr_ok", "tr_ok"))
        pta_ok, ptd_ok, pv_ok, ohi_ok, olo_ok = (sem(n) for n in ("pta_ok", "ptd_ok", "pv_ok", "ohi_ok", "olo_ok"))
        sig_ok, br_ok, sum_ok, mhi_ok, mlo_ok = (sem(n) for n in ("sig_ok", "br_ok", "sum_ok", "mhi_ok", "mlo_ok"))
        om_ok, xo_ok = sem("om_ok"), sem("xo_ok")
        h2_ok, h2hi_ok, h2tr_ok, h2ta_ok, lg_ok, lgd_ok = (sem(n) for n in ("h2_ok", "h2hi_ok", "h2tr_ok", "h2ta_ok", "lg_ok", "lgd_ok"))
        rd_ok, ra_ok, rk_ok, route_ok = (sem(n) for n in ("rd_ok", "ra_ok", "rk_ok", "route_ok"))
        gu_ld, dn_ld = [sem("gu_ld0"), sem("gu_ld1")], [sem("dn_ld0"), sem("dn_ld1")]
        sel_ok, ga_ok, xga_ok, xgd_ok, xgt_ok, xta_ok, xtd_ok = (sem(n) for n in ("sel_ok", "ga_ok", "xga_ok", "xgd_ok", "xgt_ok", "xta_ok", "xtd_ok"))
        gu_ok, sil_ok, z_ok, zt_ok, zte_ok, dn_ok, ya_ok, yd_ok = (sem(n) for n in ("gu_ok", "sil_ok", "z_ok", "zt_ok", "zte_ok", "dn_ok", "ya_ok", "yd_ok"))
        ix_ok, inf_ok, ov_inf = sem("ix_ok"), sem("inf_ok"), sem("ov_inf")
        ysc = [sem("ysc0"), sem("ysc1")]
        yl_ld = [sem(f"yl_ld{t}") for t in range(TT)]
        fin_ok, out_st = sem("fin_ok"), sem("out_st")
        ov_ld, ov_sel, ov_ga, ov_xg, ov_xt, ov_xe, ov_gu, ov_sil, ov_z, ov_zt, ov_ze, ov_dn, ov_y, ov_sc = (
            sem("ov_" + n) for n in ("ld", "sel", "ga", "xg", "xt", "xe", "gu", "sil", "z", "zt", "ze", "dn", "y", "sc"))

        ahead = {hi_ok: 1, lo_ok: 1, dn_ok: 1, z_ok: 1, ya_ok: 1, yd_ok: 1, sig_ok: 1, br_ok: 1, mlo_ok: 1, pv_ok: 1,
                 mx_ok: 1, pj_dve: 1, ysc[0]: 16, ysc[1]: 16, ov_sc: 16}

        MASK_PARTS = ((ysc[0], 0, MA), (ysc[1], MA, MA + 2 * T), (ov_sc, MA + 2 * T, MA + TT * T + 2 * P))

        def need(eng, s, value):
            eng.wait_ge(s, value + ahead[s])

        held = {e.engine: sem(f"held_{n}") for n, e in
                (("sp", nc.sync), ("act", nc.scalar), ("pe", nc.tensor), ("dve", nc.vector), ("pool", nc.gpsimd))}

        block = ctx.enter_context(nc.Block())

        def by_residue(ap):
            return ap.rearrange("p (a c r) -> p r c a", c=4, r=4)

        def in_order(ap):
            return ap.rearrange("p (r c a) -> p r c a", r=4, c=4)

        def hold(eng, s, value):
            eng.wait_ge(s, value)
            eng.sem_inc(held[eng.engine], 1)

        def overflow(eng, l, body):
            hold(eng, route_ok, l + 1)
            extra = eng.value_load(rounds_i[0:1, bass.ds(2 * l, 1)], min_val=0, max_val=7)
            before = eng.value_load(rounds_i[0:1, bass.ds(2 * l + 1, 1)], min_val=0, max_val=7 * PAIRS * 2)
            with eng.If(extra > 0):
                with eng.Fori(0, extra) as r:
                    with eng.Fori(0, PAIRS) as p:
                        body(r, p, before + r * PAIRS + p)

        @block.sync
        def _(sp):
            for t in range(TT):
                sp.dma_start(x[:, t, :], x_in[t * P:(t + 1) * P, :]).then_inc(x_ld, 16)

            def load_tile(l, i):
                if i >= 2:
                    need(sp, hi_ok, l * NT + i - 1)
                    need(sp, lo_ok, l * NT + i - 1)
                else:
                    need(sp, hi_ok, l * NT)
                    need(sp, lo_ok, l * NT)
                sp.dma_start(raw[:, i % 2, :], stream[bass.ds(l, 1), i, :, :].rearrange("o p n -> p (o n)")).then_inc(raw_ld[i % 2], 16)

            def load_gu(l, p, s):
                sp.dma_start(gu[s][:, :, :, :].rearrange("p e k n -> p e (k n)"),
                             gu_w[bass.ds(l * PAIRS + p, 1), :, :, :].rearrange("o e p n -> p (o e) n")).then_inc(gu_ld[s], 16)

            def load_dn(l, p, s):
                sp.dma_start(dn[s][:, :, :, :].rearrange("p e k n -> p e (k n)"),
                             dn_w[bass.ds(l * PAIRS + p, 1), :, :, :].rearrange("o e p n -> p (o e) n")).then_inc(dn_ld[s], 16)

            with sp.Fori(0, L) as l:
                for i in range(NT):
                    load_tile(l, i)
                    if i == NQ:
                        need(sp, dn_ok, l * PAIRS)
                        load_gu(l, 0, 0)
                        load_dn(l, 0, 0)
                sp.wait_ge(w_used, l * NT + NQ + NGATE)
                load_gu(l, 1, 1)
                load_dn(l, 1, 1)
                with sp.Fori(1, PAIRS // 2) as it:
                    for s in range(2):
                        sp.wait_ge(gu_ok, l * PAIRS + 2 * it + s - 1)
                        load_gu(l, 2 * it + s, s)
                        need(sp, dn_ok, l * PAIRS + 2 * it + s - 1)
                        load_dn(l, 2 * it + s, s)


                def more_experts(r, p, q):
                    need(sp, dn_ok, (l + 1) * PAIRS)
                    need(sp, ov_sc, q * 16)
                    sp.dma_start(gu[0][:, :, :, :].rearrange("p e k n -> p e (k n)"),
                                 gu_w[bass.ds(l * PAIRS + p, 1), :, :, :].rearrange("o e p n -> p (o e) n")).then_inc(ov_ld, 16)
                    sp.dma_start(dn[0][:, :, :, :].rearrange("p e k n -> p e (k n)"),
                                 dn_w[bass.ds(l * PAIRS + p, 1), :, :, :].rearrange("o e p n -> p (o e) n")).then_inc(ov_ld, 16)

                overflow(sp, l, more_experts)
                for s in range(2):
                    need(sp, ysc[s], (l + 1) * PAIRS * 8)
                total = sp.value_load(rounds_i[0:1, bass.ds(2 * l + 3, 1)], min_val=0, max_val=7 * PAIRS * 2)
                need(sp, ov_sc, total * 16)
                for t in range(TT):
                    for k in range(2):
                        sp.dma_start(yld[:, k, t, :], y_rows[k * T + t * P:k * T + (t + 1) * P, :]).then_inc(yl_ld[t], 16)
            for t in range(TT):
                sp.wait_ge(fin_ok, t + 1)
                sp.dma_start(out[t * P:(t + 1) * P, :], yld[:, 0, t, :]).then_inc(out_st, 16)
            sp.wait_ge(out_st, TT * 16)

        @block.tensor
        def _(pe):
            mm = nc.tensor.matmul

            def three(dst, a, b, start, stop):
                (ah, al), (bh, bl) = a, b
                mm(dst, ah, bh, start=start, stop=False)
                mm(dst, ah, bl, start=False, stop=False)
                return mm(dst, al, bh, start=False, stop=stop)

            def wt(i, k, n=P):
                s = i % 2
                return w_hi[s][:, k * n:(k + 1) * n], w_lo[s][:, k * n:(k + 1) * n]

            def project(dst, i, k0=0, src=(h_hi, h_lo), kn=KD):
                for k in range(kn):
                    last = three(dst, wt(i, k0 + k), (src[0][:, k, :], src[1][:, k, :]), k == 0, k == kn - 1)
                return last

            for s in (dn_ok, pv_ok):
                pe.sem_inc(s, ahead[s])
            pe.wait_ge(cst_ld, 16)
            with pe.Fori(0, L) as l:
                pe.wait_ge(xn_ok, l * 4 + 4)
                for k in range(KD):
                    for t in range(TT):
                        last = nc.tensor.transpose(bank[k][:, t * P:(t + 1) * P], xn[:, t, k * P:(k + 1) * P], ident)
                    last.then_inc(xt_ok, 1)
                pe.wait_ge(hlo_ok, l * KD + KD)

                def qkv_tile(i, l=l):
                    need(pe, lo_ok, l * NT + i + 1)
                    if i >= 2:
                        pe.wait_ge(pj_act, l * NQ + i - 1)
                        need(pe, pj_dve, l * ROPES[NQ] + ROPES[i - 1])
                    last = project(bank[6 + i % 2][:, :], i)
                    last.then_inc(w_used, 1)

                def transpose_v(i, l=l):
                    n = VS[i]
                    pe.wait_ge(pj_act, l * NQ + i + 1)
                    if n >= 2:
                        pe.wait_ge(v_ok, l * VS[NQ] + n - 1)
                    for t in range(TT):
                        last = nc.tensor.transpose(bank[4 + n % 2][:, t * P:(t + 1) * P], vt[:, n % 2, t * P:(t + 1) * P], ident)
                    last.then_inc(vt_ok, 1)

                def scores(u, l=l):
                    need(pe, mx_ok, l * STEPS + max(0, u - 1 if u < NSTEP_A else u))
                    for h in range(2):
                        rows = slice(h * DH, (h + 1) * DH)
                        if u < NSTEP_A:
                            j, t = divmod(u, TT)
                            k0, k1 = max(0, t - 1), min(TT, t + 2)
                            last = mm(bank[2 * (u % 2) + h][:, 0:(k1 - k0) * P], qk_a[rows, j, t * P:(t + 1) * P],
                                      qk_a[rows, 4, k0 * P:k1 * P], start=True, stop=True)
                    if u >= NSTEP_A:
                        r = (u - NSTEP_A) % TT
                        cols = slice(r * P, (r + 1) * P)
                        for h in range(2):
                            rows = slice(h * DH, (h + 1) * DH)
                            mm(bank[2 * h][:, :], qk_b[rows, 0, cols], qk_b[rows, 1, :], start=True, stop=True)
                        for g in (1, 2):
                            for h in range(2):
                                rows = slice(h * DH, (h + 1) * DH)
                                last = mm(bank[2 * h + 1][:, (g - 1) * P:g * P], qk_b[rows, 2 * g, cols],
                                          qk_b[rows, 2 * g + 1, cols], start=True, stop=True)
                    last.then_inc(sc_ok, 1)

                def transposes(u, l=l):
                    pe.wait_ge(pr_ok, l * STEPS + u + 1)
                    s = u % 2
                    if u < NSTEP_A:
                        t = u % TT
                        n = min(TT, t + 2) - max(0, t - 1)
                        for h in range(2):
                            for k in range(n):
                                last = nc.tensor.transpose(bank[4 + h][:, k * P:(k + 1) * P], prob[:, s, h, k * P:(k + 1) * P], ident)
                    else:
                        for h in range(2):
                            for k in range(TT):
                                nc.tensor.transpose(bank[4 + h][:, k * P:(k + 1) * P], prob[:, s, h, k * P:(k + 1) * P], ident)
                        for h in range(2):
                            for k in range(2):
                                last = nc.tensor.transpose(bank[6][:, (2 * h + k) * P:(2 * h + k + 1) * P],
                                                           prob[:, s, h, T + k * P:T + (k + 1) * P], ident)
                    last.then_inc(tr_ok, 1)

                def values(u, l=l):
                    pe.wait_ge(pta_ok, l * STEPS + u + 1)
                    pe.wait_ge(ptd_ok, l * STEPS + u + 1)
                    t = u % TT
                    pair = u // TT
                    if t == 0 and pair:
                        pe.wait_ge(ohi_ok, l * 6 + pair)
                        pe.wait_ge(olo_ok, l * 6 + pair)
                    cols = slice(t * P, (t + 1) * P)
                    if u < NSTEP_A:
                        k0, k1 = max(0, t - 1), min(TT, t + 2)
                        terms = [(lambda h, k=k: v_a[:, k, h * DH:(h + 1) * DH], (k - k0) * P) for k in range(k0, k1)]
                    else:
                        terms = [(lambda h, k=k: v_b[:, 0, k, h * DH:(h + 1) * DH], k * P) for k in range(TT)]
                        terms += [(lambda h, g=g: v_b[:, g, t, h * DH:(h + 1) * DH], T + (g - 1) * P) for g in (1, 2)]
                    for n, (v, c0) in enumerate(terms):
                        for h in range(2):
                            last = mm(bank[7][h * DH:(h + 1) * DH, cols], v(h), pt[:, h, c0:c0 + P],
                                      start=n == 0, stop=n == len(terms) - 1)
                    last.then_inc(pv_ok, 1)

                for b, blk in enumerate(BLOCKS):
                    if b:
                        pe.wait_ge(ohi_ok, l * 6 + 3 + b)
                        pe.wait_ge(olo_ok, l * 6 + 3 + b)
                    for n, (kind, _i) in enumerate(blk):
                        qkv_tile(BLOCK_AT[b] + n)
                        if n >= 1 and blk[n - 1][0] == V:
                            transpose_v(BLOCK_AT[b] + n - 1)
                    end = BLOCK_AT[b] + len(blk)
                    pe.wait_ge(rope_ok, l * ROPES[NQ] + ROPES[end])
                    pe.wait_ge(v_ok, l * VS[NQ] + VS[end])
                    u0, u1 = (0, NSTEP_A) if b == 0 else (NSTEP_A + 4 * (b - 1), NSTEP_A + 4 * b)
                    scores(u0)
                    scores(u0 + 1)
                    for u in range(u0, u1):
                        transposes(u)
                        if u + 2 < u1:
                            scores(u + 2)
                        values(u)

                hold(pe, olo_ok, l * 6 + 6)
                with pe.Fori(0, KD // 2) as it:
                    for half in range(2):
                        b4 = 4 * half
                        i0 = NQ + 3 * half
                        n = l * NT + it * 6 + i0
                        need(pe, sig_ok, l * 2 * KD + it * 4 + 2 * half)
                        need(pe, br_ok, l * KD + it * 2 + half)
                        for gte in range(2):
                            need(pe, lo_ok, n + gte + 1)
                            project(bank[b4 + gte][:, :], i0 + gte).then_inc(w_used, 1)
                        need(pe, lo_ok, n + 3)
                        project(bank[b4 + 2][:, :], i0 + 2, 0, (o_hi, o_lo), 4)
                        for k in range(2):
                            last = three(bank[b4 + 3][:, :], wt(i0 + 2, 4 + k), (o_hi[:, 4 + k, :], o_lo[:, 4 + k, :]), k == 0, k == 1)
                        last.then_inc(w_used, 1)

                pe.wait_ge(mhi_ok, l * KD + KD)
                need(pe, mlo_ok, l * KD + KD + 1)
                need(pe, br_ok, l * KD + KD + 1)
                for dh in range(2):
                    for kp in range(4):
                        i = NQ + NGATE + dh * 4 + kp
                        need(pe, lo_ok, l * NT + i + 1)
                        for t in range(TT):
                            for kk in range(2):
                                k = 2 * kp + kk
                                wh, wl = wt(i, kk, 512)
                                tok = slice(t * P, (t + 1) * P)
                                last = three(bank[4 * dh + t][:, :], (m_hi[:, k, tok], m_lo[:, k, tok]), (wh, wl), k == 0, k == KD - 1)
                            if kp == 3 and t < TT - 1:
                                last.then_inc(om_ok, 1)
                        last.then_inc(w_used, 1)

                for t in range(TT):
                    pe.wait_ge(h2_ok, l * TT + t + 1)
                    if t >= 2:
                        pe.wait_ge(h2ta_ok, l * TT + t - 1)
                    for k in range(KD):
                        last = nc.tensor.transpose(bank[2 * (t % 2) + k // 4][:, (k % 4) * P:(k % 4 + 1) * P],
                                                   xn2[:, t % 2, k * P:(k + 1) * P], ident)
                    last.then_inc(h2tr_ok, 1)
                for t in range(TT):
                    pe.wait_ge(h2ta_ok, l * TT + t + 1)
                    for k in range(KD):
                        last = mm(bank[4][:, t * NLOG:(t + 1) * NLOG], h2t[:, k, t * P:(t + 1) * P], wr[:, k, :],
                                  start=k == 0, stop=k == KD - 1)
                last.then_inc(lg_ok, 1)
                pe.wait_ge(rk_ok, l + 1)
                for t in range(TT + 1):
                    for s in range(min(t + 1, TT)):
                        last = mm(bank[5][:, t * NE:(t + 1) * NE], c(C_TRI, P) if s == t else c(C_ONE, P), asg[:, s, :],
                                  start=s == 0, stop=s == min(t, TT - 1))
                last.then_inc(lgd_ok, 1)

                def gather(s, e0, info_done, done):
                    for t in range(TT):
                        last = mm(bank[5][:, 2 * P:2 * P + 4], sel[:, s, t, :].bitcast(FP32), info[:, t, :, bass.ds(e0, 2)],
                                  start=t == 0, stop=t == TT - 1)
                    last.then_inc(info_done, 1)
                    for t in range(TT):
                        for half in range(2):
                            for n, part in enumerate((h2_hi, h2_lo)):
                                last = mm(bank[half][:, :], sel[:, s, t, :], part[:, t, half * T:(half + 1) * T],
                                          start=t == 0 and n == 0, stop=t == TT - 1 and n == 1)
                    last.then_inc(done, 1)

                def turn(done):
                    for k in range(KD):
                        last = nc.tensor.transpose(bank[2 + k // 4][:, (k % 4) * P:(k % 4 + 1) * P], xg[:, k * P:(k + 1) * P], ident)
                    last.then_inc(done, 1)

                def up(s, done):
                    for k in range(KD):
                        for e in range(2):
                            last = mm(bank[4][e * CAP:(e + 1) * CAP, :], xgt[:, k, e * CAP:(e + 1) * CAP], gu[s][:, e, k, :],
                                      start=k == 0, stop=k == KD - 1)
                    last.then_inc(done, 1)

                def turn_z(done):
                    for f in range(2):
                        last = nc.tensor.transpose(bank[5][:, f * P:(f + 1) * P], z[:, f * P:(f + 1) * P], ident)
                    last.then_inc(done, 1)

                def down(s, done):
                    for half in range(2):
                        for f in range(2):
                            for e in range(2):
                                last = mm(bank[6 + half][e * CAP:(e + 1) * CAP, :], zt[:, f, e * CAP:(e + 1) * CAP],
                                          dn[s][:, e, f, half * T:(half + 1) * T], start=f == 0, stop=f == 1)
                    last.then_inc(done, 1)

                n0 = l * PAIRS
                pe.wait_ge(sel_ok, n0 + 1)
                gather(0, 0, inf_ok, ga_ok)
                pe.wait_ge(xga_ok, n0 + 1)
                pe.wait_ge(xgd_ok, n0 + 1)
                turn(xgt_ok)

                def pair(it, s, last_pair=False):
                    n = n0 + 2 * it + s
                    pe.wait_ge(xta_ok, n + 1)
                    pe.wait_ge(xtd_ok, n + 1)
                    pe.wait_ge(gu_ld[s], (l * (PAIRS // 2) + it + 1) * 16)
                    need(pe, z_ok, n)
                    up(s, gu_ok)
                    if not last_pair:
                        pe.wait_ge(sel_ok, n + 2)
                        gather(1 - s, 2 * (2 * it + s + 1), inf_ok, ga_ok)
                    need(pe, z_ok, n + 1)
                    if not last_pair:
                        pe.wait_ge(ix_ok, n + 2)
                    turn_z(zt_ok)
                    if not last_pair:
                        pe.wait_ge(xga_ok, n + 2)
                        pe.wait_ge(xgd_ok, n + 2)
                        turn(xgt_ok)
                    pe.wait_ge(zte_ok, n + 1)
                    pe.wait_ge(dn_ld[s], (l * (PAIRS // 2) + it + 1) * 16)
                    need(pe, ya_ok, n)
                    need(pe, yd_ok, n)
                    down(s, dn_ok)

                with pe.Fori(0, PAIRS // 2 - 1) as it:
                    pair(it, 0)
                    pair(it, 1)
                pair(PAIRS // 2 - 1, 0)
                pair(PAIRS // 2 - 1, 1, True)


                def more_experts(r, p, q):
                    need(pe, ya_ok, n0 + PAIRS)
                    need(pe, yd_ok, n0 + PAIRS)
                    pe.wait_ge(ov_sel, q + 1)
                    gather(0, 2 * p, ov_inf, ov_ga)
                    pe.wait_ge(ov_xg, q + 1)
                    turn(ov_xt)
                    pe.wait_ge(ov_xe, q + 1)
                    pe.wait_ge(ov_ld, (q + 1) * 32)
                    up(0, ov_gu)
                    pe.wait_ge(ov_z, q + 1)
                    turn_z(ov_zt)
                    pe.wait_ge(ov_ze, q + 1)
                    down(0, ov_dn)
                    pe.wait_ge(ov_y, q + 1)

                overflow(pe, l, more_experts)

        @block.scalar
        def _(act):
            run = nc.scalar.activation
            act.dma_start(cst[:, :], consts).then_inc(cst_ld, 16)
            for s in (hi_ok, ya_ok):
                act.sem_inc(s, ahead[s])
            act.sem_inc(sig_ok, ahead[sig_ok] + 2)

            def split_hi(l, i, it=0):
                act.wait_ge(raw_ld[i % 2], (l * (NT // 2) + it * 3 + i // 2 + 1) * 16)
                if i >= 2:
                    act.wait_ge(w_used, l * NT + it * 6 + i - 1)
                run(w_hi[i % 2][:, :], raw[:, i % 2, :], ACT.Copy).then_inc(hi_ok, 1)

            def squares(l_tiles, dst):
                for t in range(TT):
                    l_tiles(t)
                    run(dst(t), x[:, t, :], ACT.Square, accum_out=ss[:, t:t + 1]).then_inc(sq_ok, 1)

            def root(n):
                act.wait_ge(ms_ok, n + 1)
                run(rs, ms, ACT.Sqrt).then_inc(rt_ok, 1)

            with act.Fori(0, L) as l:
                squares(lambda t: act.wait_ge(x_ok, l * TT + t + 1), lambda t: xn[:, t, :])
                root(2 * l)
                split_hi(l, 0)
                split_hi(l, 1)
                act.wait_ge(par_ld, (l + 1) * 16)
                for k in range(KD):
                    act.wait_ge(xt_ok, l * KD + k + 1)
                    run(h_hi[:, k, :], bank[k][:, :], ACT.Identity, scale=g_col[:, k:k + 1]).then_inc(hhi_ok, 1)

                def epilogue(i, l=l):
                    _b, kind, idx = QKV[i]
                    act.wait_ge(w_used, l * NT + i + 1)
                    src = bank[6 + i % 2]
                    if kind == V:
                        n = VS[i]
                        if n >= 2:
                            act.wait_ge(vt_ok, l * VS[NQ] + n - 1)
                        if _b and idx:
                            run(in_order(vt[:, n % 2, :]), by_residue(src[:, :]), ACT.Copy).then_inc(pj_act, 1)
                        else:
                            run(vt[:, n % 2, :], src[:, :], ACT.Copy).then_inc(pj_act, 1)
                        return
                    r = ROPES[i]
                    if r >= 2:
                        act.wait_ge(rope_ok, l * ROPES[NQ] + r - 1)
                    need(act, pj_dve, l * ROPES[NQ] + r + 1)
                    for q in range(4):
                        last = run(swp[q * 32:q * 32 + 32, r % 2, :], src[(q ^ 1) * 32:(q ^ 1) * 32 + 32, :], ACT.Copy)
                    last.then_inc(pj_act, 1)

                def width(u):
                    t = u % TT
                    return (min(TT, t + 2) - max(0, t - 1)) * P if u < NSTEP_A else MB

                def exps(u, l=l):
                    need(act, mx_ok, l * STEPS + u + 1)
                    s = u % 2
                    if u < NSTEP_A:
                        run(es[:, 2 * s:2 * s + 2], nm2[:, 2 * s:2 * s + 2], ACT.Exp)
                    for h in range(2):
                        p = prob[:, s, h, 0:width(u)]
                        last = run(p, p, ACT.Exp, bias=nmx[:, 2 * s + h:2 * s + h + 1], scale=-1.0,
                                   accum_out=rsum[:, 2 * s + h:2 * s + h + 1])
                    last.then_inc(ex_ok, 1)

                def copy_pt(u, l=l):
                    act.wait_ge(tr_ok, l * STEPS + u + 1)
                    need(act, pv_ok, l * STEPS + u)
                    if u < NSTEP_A:
                        run(pt[:, 0, 0:width(u)], bank[4][:, 0:width(u)], ACT.Copy).then_inc(pta_ok, 1)
                    else:
                        run(pt[:, 0, 0:T], bank[4][:, :], ACT.Copy)
                        run(pt[:, :, T:MB], bank[6][:, :].rearrange("p (h n) -> p h n", h=2), ACT.Copy).then_inc(pta_ok, 1)

                def copy_o(pair, l=l):
                    need(act, pv_ok, l * STEPS + 4 * pair + 4)
                    if pair < 4:
                        run(o_hi[:, pair, :], bank[7][:, :], ACT.Copy).then_inc(ohi_ok, 1)
                    else:
                        run(by_residue(o_hi[:, pair, :]), in_order(bank[7][:, :]), ACT.Copy).then_inc(ohi_ok, 1)

                for b, blk in enumerate(BLOCKS):
                    for n in range(len(blk)):
                        i = BLOCK_AT[b] + n
                        if i:
                            split_hi(l, i + 1)
                        epilogue(i)
                    u0, u1 = (0, NSTEP_A) if b == 0 else (NSTEP_A + 4 * (b - 1), NSTEP_A + 4 * b)
                    exps(u0)
                    exps(u0 + 1)
                    for u in range(u0, u1):
                        copy_pt(u)
                        if u + 2 < u1:
                            exps(u + 2)
                        if u % TT == TT - 1:
                            copy_o(u // TT)

                with act.Fori(0, KD // 2) as it:
                    for half in range(2):
                        i0 = NQ + 3 * half
                        for gte in range(2):
                            split_hi(l, i0 + gte + 1, it)
                            act.wait_ge(w_used, l * NT + it * 6 + i0 + gte + 1)
                            if gte == 0:
                                need(act, br_ok, l * KD + it * 2 + half)
                            run(sg[:, half, gte, :], bank[4 * half + gte][:, :], ACT.Sigmoid).then_inc(sig_ok, 1)
                        split_hi(l, i0 + 3, it)
                        act.wait_ge(sum_ok, l * KD + it * 2 + half + 1)
                        run(m_hi[:, bass.ds(it * 2 + half, 1), :].rearrange("p o n -> p (o n)"), mab[:, half, 0, :], ACT.Copy).then_inc(mhi_ok, 1)
                for i in range(NQ + NGATE + 1, NT):
                    split_hi(l, i)

                squares(lambda t: act.wait_ge(xo_ok, l * 8 + 5 + t), lambda t: junk[:, t, :])
                root(2 * l + 1)
                for t in range(TT):
                    act.wait_ge(h2_ok, l * TT + t + 1)
                    run(h2_hi[:, t, :], xn2[:, t % 2, :], ACT.Copy).then_inc(h2hi_ok, 1)
                    act.wait_ge(h2tr_ok, l * TT + t + 1)
                    for kh in range(2):
                        last = run(h2t[:, 4 * kh:4 * kh + 4, t * P:(t + 1) * P],
                                   bank[2 * (t % 2) + kh][:, :].rearrange("p (k n) -> p k n", k=4), ACT.Copy)
                    last.then_inc(h2ta_ok, 1)
                act.wait_ge(rd_ok, 2 * l + 1)
                run(ge, ge, ACT.Exp).then_inc(ra_ok, 1)
                act.wait_ge(rd_ok, 2 * l + 2)
                run(wts[:, :, 3:4], wts[:, :, 2:3], ACT.Exp).then_inc(ra_ok, 1)

                n0 = l * PAIRS

                def first_half(n):
                    act.wait_ge(ga_ok, n + 1)
                    run(xg[:, 0:T], bank[0][:, :], ACT.Copy).then_inc(xga_ok, 1)

                def turned(n):
                    act.wait_ge(xgt_ok, n + 1)
                    run(xgt[:, 0:4, :], bank[2][:, :].rearrange("p (k n) -> p k n", k=4), ACT.Copy).then_inc(xta_ok, 1)

                def pair(it, s, last_pair=False):
                    n = n0 + 2 * it + s
                    act.wait_ge(gu_ok, n + 1)
                    run(sil[:, :], bank[4][:, 0:FE], ACT.Silu).then_inc(sil_ok, 1)
                    if not last_pair:
                        first_half(n + 1)
                    act.wait_ge(zt_ok, n + 1)
                    need(act, dn_ok, n)
                    run(zt[:, :, :], bank[5][:, 0:FE].rearrange("p (f n) -> p f n", f=2), ACT.Copy).then_inc(zte_ok, 1)
                    if not last_pair:
                        turned(n + 1)
                    need(act, dn_ok, n + 1)
                    act.wait_ge(ix_ok, n + 1)
                    need(act, ysc[s], (l * (PAIRS // 2) + it) * 16)
                    run(yb[:, s, 0:T], bank[6][:, :], ACT.Identity, scale=wslot[:, s:s + 1]).then_inc(ya_ok, 1)

                first_half(n0)
                turned(n0)
                with act.Fori(0, PAIRS // 2 - 1) as it:
                    pair(it, 0)
                    pair(it, 1)
                pair(PAIRS // 2 - 1, 0)
                pair(PAIRS // 2 - 1, 1, True)

                def more_experts(r, p, q):
                    act.wait_ge(ov_gu, q + 1)
                    run(sil[:, :], bank[4][:, 0:FE], ACT.Silu).then_inc(ov_sil, 1)

                overflow(act, l, more_experts)
            squares(lambda t: act.wait_ge(x_ok, L * TT + t + 1), lambda t: yld[:, 0, t, :])
            root(2 * L)

        @block.vector
        def _(dve):
            v = nc.vector
            tt, ts, stt = v.tensor_tensor, v.tensor_scalar, v.scalar_tensor_tensor
            for s, _a, _b in MASK_PARTS:
                dve.wait_ge(s, ahead[s])
            dve.wait_ge(cst_ld, 16)
            v.tensor_copy(mask_a[:, :], mask_f32[:, 0:MA])
            v.tensor_copy(mask_b[:, :, :], mask_f32[:, MA:MA + TT * T].rearrange("p (r n) -> p r n", n=T))
            v.tensor_copy(mask_b12[:, :], mask_f32[:, MA + TT * T:MA + TT * T + 2 * P])
            v.memset(rounds_i[0:1, :], 0)
            v.memset(rounds_f[:, :], 0.0)
            for s in (lo_ok, z_ok, yd_ok, mx_ok, pj_dve):
                dve.sem_inc(s, ahead[s])
            dve.sem_inc(br_ok, ahead[br_ok] + 1)
            v.drain()
            dve.wait_ge(x_ld, TT * 16)
            dve.sem_inc(x_ok, TT)

            def split_lo(l, i, it=0):
                need(dve, hi_ok, l * NT + it * 6 + i + 1)
                tt(w_lo[i % 2][:, :], raw[:, i % 2, :], w_hi[i % 2][:, :].bitcast(FP32), ALU.subtract).then_inc(lo_ok, 1)

            def rstd(n):
                dve.wait_ge(sq_ok, (n + 1) * TT)
                ts(ms, ss, 1.0 / D, EPS, ALU.mult, ALU.add).then_inc(ms_ok, 1)
                dve.wait_ge(rt_ok, n + 1)
                v.reciprocal(nt1, rs)
                v.drain()
                tt(nt2, nt1, nt1, ALU.mult)
                v.drain()
                tt(nt2, nt2, ms, ALU.mult)
                v.drain()
                ts(nt2, nt2, -0.5, 1.5, ALU.mult, ALU.add)
                v.drain()
                tt(rs, nt1, nt2, ALU.mult)
                v.drain()

            with dve.Fori(0, L) as l:
                rstd(2 * l)
                for t in range(TT):
                    ts(xn[:, t, :], x[:, t, :], rs[:, t:t + 1], None, ALU.mult).then_inc(xn_ok, 1)
                split_lo(l, 0)
                split_lo(l, 1)
                for k in range(KD):
                    dve.wait_ge(hhi_ok, l * KD + k + 1)
                    stt(h_lo[:, k, :], bank[k][:, :], g_col[:, k:k + 1], h_hi[:, k, :].bitcast(FP32), ALU.mult,
                        ALU.subtract).then_inc(hlo_ok, 1)

                def epilogue(i, l=l):
                    b, kind, idx = QKV[i]
                    if kind == V:
                        return
                    r = ROPES[i]
                    dve.wait_ge(w_used, l * NT + i + 1)
                    if r >= 2:
                        dve.wait_ge(rope_ok, l * ROPES[NQ] + r - 1)
                    tt(rca[:, r % 2, :], bank[6 + i % 2][:, :], c(C_COS, T), ALU.mult).then_inc(pj_dve, 1)

                def copy_v(i, l=l):
                    b, kind, idx = QKV[i]
                    n = VS[i]
                    dve.wait_ge(vt_ok, l * VS[NQ] + n + 1)
                    dst = v_b[:, idx, :, :] if b else v_a[:, :, :]
                    v.tensor_copy(dst, bank[4 + n % 2][:, :].rearrange("p (t n) -> p t n", t=TT)).then_inc(v_ok, 1)

                def maxima(u, l=l):
                    hold(dve, sc_ok, l * STEPS + u + 1)
                    s = u % 2
                    for h in range(2):
                        m = nmx[:, 2 * s + h:2 * s + h + 1]
                        if u < NSTEP_A:
                            j, t = divmod(u, TT)
                            k0, k1 = max(0, t - 1), min(TT, t + 2)
                            n = (k1 - k0) * P
                            c0 = (k0 - t + 1) * P
                            v.tensor_tensor_reduce(out=prob[:, s, h, 0:n], in0=bank[2 * (u % 2) + h][:, 0:n], in1=mask_a[:, c0:c0 + n],
                                                   scale=-SCALE, scalar=nsink[:, 2 * j + h:2 * j + h + 1], op0=ALU.add, op1=ALU.min, accum_out=m)
                        else:
                            r = (u - NSTEP_A) % TT
                            v.tensor_tensor_reduce(out=prob[:, s, h, 0:T], in0=bank[2 * h][:, :], in1=mask_b[:, r, :],
                                                   scale=-SCALE, scalar=3.0e38, op0=ALU.add, op1=ALU.min, accum_out=m)
                            v.tensor_tensor_reduce(out=prob[:, s, h, T:MB], in0=bank[2 * h + 1][:, 0:2 * P], in1=mask_b12[:, :],
                                                   scale=-SCALE, scalar=3.0e38, op0=ALU.add, op1=ALU.min,
                                                   accum_out=nm2[:, 2 * s + h:2 * s + h + 1])
                    v.drain()
                    two = slice(2 * s, 2 * s + 2)
                    if u < NSTEP_A:
                        tt(nm2[:, two], nmx[:, two], sink[:, 2 * j:2 * j + 2], ALU.add).then_inc(mx_ok, 1)
                    else:
                        tt(nmx[:, two], nmx[:, two], nm2[:, two], ALU.min).then_inc(mx_ok, 1)

                def normalise(u, l=l):
                    dve.wait_ge(ex_ok, l * STEPS + u + 1)
                    s = u % 2
                    two = slice(2 * s, 2 * s + 2)
                    if u < NSTEP_A:
                        t = u % TT
                        n = (min(TT, t + 2) - max(0, t - 1)) * P
                        tt(den[:, two], rsum[:, two], es[:, two], ALU.add)
                        v.drain()
                        v.reciprocal(den[:, two], den[:, two])
                    else:
                        n = MB
                        v.reciprocal(den[:, two], rsum[:, two])
                    v.drain()
                    for h in range(2):
                        p = prob[:, s, h, 0:n]
                        last = ts(p, p, den[:, 2 * s + h:2 * s + h + 1], None, ALU.mult)
                    last.then_inc(pr_ok, 1)

                def copy_pt(u, l=l):
                    dve.wait_ge(tr_ok, l * STEPS + u + 1)
                    need(dve, pv_ok, l * STEPS + u)
                    t = u % TT
                    n = (min(TT, t + 2) - max(0, t - 1)) * P if u < NSTEP_A else T
                    v.tensor_copy(pt[:, 1, 0:n], bank[5][:, 0:n]).then_inc(ptd_ok, 1)

                def copy_o(pair, l=l):
                    dve.wait_ge(ohi_ok, l * 6 + pair + 1)
                    hi, lo, src = o_hi[:, pair, :].bitcast(FP32), o_lo[:, pair, :], bank[7][:, :]
                    if pair >= 4:
                        hi, lo, src = by_residue(hi), by_residue(lo), in_order(src)
                    tt(lo, src, hi, ALU.subtract).then_inc(olo_ok, 1)

                dve.wait_ge(par_ld, (l + 1) * 16)
                ts(nsink[:, :], sink, -1.0, None, ALU.mult)
                for b, blk in enumerate(BLOCKS):
                    for n in range(len(blk)):
                        i = BLOCK_AT[b] + n
                        if i:
                            split_lo(l, i + 1)
                        if n >= 2 and blk[n - 2][0] == V:
                            copy_v(i - 2)
                        epilogue(i)
                    u0, u1 = (0, NSTEP_A) if b == 0 else (NSTEP_A + 4 * (b - 1), NSTEP_A + 4 * b)
                    maxima(u0)
                    maxima(u0 + 1)
                    normalise(u0)
                    for u in range(u0, u1):
                        copy_pt(u)
                        if u + 1 < u1:
                            normalise(u + 1)
                        if u + 2 < u1:
                            maxima(u + 2)
                        if u % TT == TT - 1:
                            copy_o(u // TT)

                with dve.Fori(0, KD // 2) as it:
                    for half in range(2):
                        i0 = NQ + 3 * half
                        for n in range(3):
                            split_lo(l, i0 + n + 1, it)
                        need(dve, sig_ok, l * 2 * KD + it * 4 + 2 * half + 4)
                        dve.wait_ge(w_used, l * NT + it * 6 + i0 + 3)
                        need(dve, mlo_ok, l * KD + it * 2 + half)
                        tt(mab[:, half, 0, :], bank[4 * half + 2][:, :], sg[:, half, 0, :], ALU.mult)
                        tt(mab[:, half, 1, :], bank[4 * half + 3][:, :], sg[:, half, 1, :], ALU.mult).then_inc(br_ok, 1)
                for i in range(NQ + NGATE + 1, NT):
                    split_lo(l, i)
                    if i == NQ + NGATE + 5:
                        dve.wait_ge(w_used, l * NT + NQ + NGATE + 4)
                        for t in range(TT):
                            tt(x[:, t, 0:T], x[:, t, 0:T], bank[t][:, :], ALU.add).then_inc(xo_ok, 1)
                for t in range(TT):
                    if t < TT - 1:
                        dve.wait_ge(om_ok, l * 6 + 4 + t)
                    else:
                        dve.wait_ge(w_used, l * NT + NT)
                    tt(x[:, t, T:D], x[:, t, T:D], bank[4 + t][:, :], ALU.add).then_inc(xo_ok, 1)

                rstd(2 * l + 1)
                dve.wait_ge(gr_ld, (l + 1) * 16)
                for t in range(TT):
                    if t >= 2:
                        dve.wait_ge(h2tr_ok, l * TT + t - 1)
                    ts(xn2[:, t % 2, :], x[:, t, :], rs[:, t:t + 1], None, ALU.mult)
                    v.drain()
                    tt(xn2[:, t % 2, :], xn2[:, t % 2, :], g_row[:, :], ALU.mult).then_inc(h2_ok, 1)
                    dve.wait_ge(h2hi_ok, l * TT + t + 1)
                    tt(h2_lo[:, t, :], xn2[:, t % 2, :], h2_hi[:, t, :].bitcast(FP32), ALU.subtract)

                dve.wait_ge(lg_ok, l + 1)
                tt(logit, bank[4][:, 0:TT * NLOG].rearrange("p (t n) -> p t n", n=NLOG),
                   br.rearrange("p (o n) -> p o n", o=1).to_broadcast([P, TT, NLOG]), ALU.add)
                v.memset(gl8, -3.0e38)
                v.drain()
                v.tensor_copy(gl8[:, :, 0:NGRP], logit[:, :, 0:NGRP])
                v.drain()
                for t in range(TT):
                    v.max(top_g[:, t, :], gl8[:, t, :])
                v.drain()
                for t in range(TT):
                    v.max_index(idx_g[:, t, :].bitcast(U32), top_g[:, t, :], gl8[:, t, :])
                tt(ge, logit[:, :, 0:NGRP], top_g[:, :, 0:1].to_broadcast([P, TT, NGRP]), ALU.subtract).then_inc(rd_ok, 1)
                v.drain()
                v.tensor_copy(idxf[:, :, 0:1], idx_g[:, :, 0:1].bitcast(U32))
                v.drain()

                def iota(n, *shape):
                    return c(C_IOTA, n)

                tt(oh_g, c(C_IOTA, NGRP).rearrange("p (o n) -> p o n", o=1).to_broadcast([P, TT, NGRP]),
                   idxf[:, :, 0:1].to_broadcast([P, TT, NGRP]), ALU.is_equal)
                v.drain()
                tt(elm, logit[:, :, NGRP:NLOG].rearrange("p t (g e) -> p t g e", e=EPG),
                   oh_g.rearrange("p t (g o) -> p t g o", o=1).to_broadcast([P, TT, NGRP, EPG]), ALU.mult)
                v.drain()
                v.tensor_reduce(el8, elm.rearrange("p t g e -> p t e g"), AX.X, ALU.add)
                v.drain()
                for t in range(TT):
                    v.max(top_e[:, t, :], el8[:, t, :])
                v.drain()
                for t in range(TT):
                    v.max_index(idx_e[:, t, :].bitcast(U32), top_e[:, t, :], el8[:, t, :])
                tt(wts[:, :, 2:3], top_e[:, :, 1:2], top_e[:, :, 0:1], ALU.subtract).then_inc(rd_ok, 1)
                v.drain()
                v.tensor_copy(idxf[:, :, 1:3], idx_e[:, :, 0:2].bitcast(U32))
                v.drain()
                for k in range(2):
                    tt(oh8[:, :, k, :], c(C_IOTA, EPG).rearrange("p (o n) -> p o n", o=1).to_broadcast([P, TT, EPG]),
                       idxf[:, :, 1 + k:2 + k].to_broadcast([P, TT, EPG]), ALU.is_equal)
                v.drain()
                for t in range(TT):
                    for k, dst in ((0, oh1), (1, oh2)):
                        tt(dst[:, t, :, :], oh_g[:, t, :].rearrange("p (g o) -> p g o", o=1).to_broadcast([P, NGRP, EPG]),
                           oh8[:, t, k:k + 1, :].to_broadcast([P, NGRP, EPG]), ALU.mult)
                v.drain()
                one = oh1.rearrange("p t g e -> p t (g e)")
                two_ = oh2.rearrange("p t g e -> p t (g e)")
                tt(asg, one, two_, ALU.add).then_inc(rk_ok, 1)
                dve.wait_ge(ra_ok, 2 * l + 2)
                v.tensor_reduce(wts[:, :, 0], ge, AX.X, ALU.add)
                ts(wts[:, :, 4:5], wts[:, :, 3:4], 1.0, None, ALU.add)
                v.drain()
                v.reciprocal(wts[:, :, 1:2], wts[:, :, 0:1])
                v.reciprocal(wts[:, :, 5:6], wts[:, :, 4:5])
                v.drain()
                tt(wts[:, :, 6:7], wts[:, :, 1:2], wts[:, :, 5:6], ALU.mult)
                v.drain()
                tt(wts[:, :, 7:8], wts[:, :, 6:7], wts[:, :, 3:4], ALU.mult)
                v.drain()
                tok = c(C_TOK, 8)
                for which, (a1, a2) in enumerate(((wts[:, :, 6:7], wts[:, :, 7:8]),
                                                  (tok[:, 0:TT].rearrange("p (t o) -> p t o", o=1), tok[:, TT:2 * TT].rearrange("p (t o) -> p t o", o=1)))):
                    tt(info[:, :, which, :], one, a1.to_broadcast([P, TT, NE]), ALU.mult)
                    tt(rtmp, two_, a2.to_broadcast([P, TT, NE]), ALU.mult)
                    v.drain()
                    tt(info[:, :, which, :], info[:, :, which, :], rtmp, ALU.add)
                    v.drain()
                dve.wait_ge(lgd_ok, l + 1)
                stt(rankm, asg, NEVER, bank[5][:, 0:TT * NE].rearrange("p (t n) -> p t n", n=NE), ALU.mult, ALU.add)
                v.tensor_reduce(cnt_s[:, 0:1], bank[5][:, TT * NE:(TT + 1) * NE], AX.X, ALU.max)
                v.drain()
                ts(rankm, rankm, -NEVER, None, ALU.add)
                ts(more[:, 0:7], c(C_THR, 7), cnt_s[:, 0:1], None, ALU.is_lt)
                v.drain()
                v.tensor_reduce(rounds_f[:, 0:1], more[:, 0:7], AX.X, ALU.add)
                v.drain()
                v.tensor_copy(rounds_i[0:1, bass.ds(2 * l, 2)], rounds_f[0:1, :])
                v.drain()
                stt(rounds_f[:, 1:2], rounds_f[:, 0:1], float(PAIRS), rounds_f[:, 1:2], ALU.mult, ALU.add)
                v.drain()
                v.tensor_copy(rounds_i[0:1, bass.ds(2 * l + 3, 1)], rounds_f[0:1, 1:2]).then_inc(route_ok, 1)

                n0 = l * PAIRS

                def choose(s, e0, done, shift=None):
                    src = rankm[:, :, bass.ds(e0, 2)]
                    for t in range(TT):
                        last = tt(sel[:, s, t, :].rearrange("p (e n) -> p e n", e=2),
                                  c(C_IOTA, CAP).rearrange("p (o n) -> p o n", o=1).to_broadcast([P, 2, CAP]),
                                  src[:, t, :].rearrange("p (e o) -> p e o", o=1).to_broadcast([P, 2, CAP]), ALU.is_equal)
                    last.then_inc(done, 1)

                def slots(s):
                    at0 = 2 * P
                    for e in range(2):
                        rows = slice(e * CAP, (e + 1) * CAP)
                        v.tensor_copy(wslot[rows, s:s + 1], bank[5][rows, at0 + e:at0 + e + 1])
                        last = ts(idx_row[rows, s:s + 1], bank[5][rows, at0 + 2 + e:at0 + 3 + e], BIG, None, ALU.add)
                    return last

                def second_half(n, s):
                    dve.wait_ge(ga_ok, n + 1)
                    v.tensor_copy(xg[:, T:D], bank[1][:, :]).then_inc(xgd_ok, 1)

                def turned(n):
                    dve.wait_ge(xgt_ok, n + 1)
                    v.tensor_copy(xgt[:, 4:8, :], bank[3][:, :].rearrange("p (k n) -> p k n", k=4)).then_inc(xtd_ok, 1)

                def pair(it, s, left=2):
                    n = n0 + 2 * it + s
                    dve.wait_ge(sil_ok, n + 1)
                    tt(z[:, :], bank[4][:, FE:2 * FE], sil[:, :], ALU.mult).then_inc(z_ok, 1)
                    if left >= 1:
                        dve.wait_ge(inf_ok, n + 2)
                        need(dve, ysc[1 - s], (l * (PAIRS // 2) + it + s) * 16)
                        slots(1 - s).then_inc(ix_ok, 1)
                        second_half(n + 1, 1 - s)
                        turned(n + 1)
                    if left >= 2:
                        choose(s, 2 * (2 * it + s + 2), sel_ok)
                    need(dve, dn_ok, n + 1)
                    need(dve, ysc[s], (l * (PAIRS // 2) + it) * 16)
                    ts(yb[:, s, T:D], bank[7][:, :], wslot[:, s:s + 1], None, ALU.mult).then_inc(yd_ok, 1)

                choose(0, 0, sel_ok)
                choose(1, 2, sel_ok)
                dve.wait_ge(inf_ok, n0 + 1)
                slots(0).then_inc(ix_ok, 1)
                second_half(n0, 0)
                turned(n0)
                with dve.Fori(0, PAIRS // 2 - 1) as it:
                    pair(it, 0)
                    pair(it, 1)
                pair(PAIRS // 2 - 1, 0, 1)
                pair(PAIRS // 2 - 1, 1, 0)

                def more_experts(r, p, q):
                    with dve.If(p == 0):
                        ts(rankm, rankm, -float(CAP), None, ALU.add)
                        v.drain()
                    need(dve, ysc[0], (l + 1) * (PAIRS // 2) * 16)
                    need(dve, ysc[1], (l + 1) * (PAIRS // 2) * 16)
                    need(dve, ov_sc, q * 16)
                    choose(0, 2 * p, ov_sel)
                    dve.wait_ge(ov_ga, q + 1)
                    v.tensor_copy(xg[:, 0:T], bank[0][:, :])
                    slots(0)
                    v.tensor_copy(xg[:, T:D], bank[1][:, :]).then_inc(ov_xg, 1)
                    dve.wait_ge(ov_xt, q + 1)
                    for kh in range(2):
                        last = v.tensor_copy(xgt[:, 4 * kh:4 * kh + 4, :], bank[2 + kh][:, :].rearrange("p (k n) -> p k n", k=4))
                    last.then_inc(ov_xe, 1)
                    dve.wait_ge(ov_sil, q + 1)
                    tt(z[:, :], bank[4][:, FE:2 * FE], sil[:, :], ALU.mult).then_inc(ov_z, 1)
                    dve.wait_ge(ov_zt, q + 1)
                    v.tensor_copy(zt[:, :, :], bank[5][:, 0:FE].rearrange("p (f n) -> p f n", f=2)).then_inc(ov_ze, 1)
                    dve.wait_ge(ov_dn, q + 1)
                    ts(yb[:, 0, 0:T], bank[6][:, :], wslot[:, 0:1], None, ALU.mult)
                    ts(yb[:, 0, T:D], bank[7][:, :], wslot[:, 0:1], None, ALU.mult).then_inc(ov_y, 1)

                overflow(dve, l, more_experts)

                for t in range(TT):
                    dve.wait_ge(yl_ld[t], (l + 1) * 32)
                    tt(yld[:, 0, t, :], yld[:, 0, t, :], yld[:, 1, t, :], ALU.add)
                    v.drain()
                    tt(x[:, t, :], x[:, t, :], yld[:, 0, t, :], ALU.add).then_inc(x_ok, 1)
            rstd(2 * L)
            dve.wait_ge(gr_ld, (L + 1) * 16)
            for t in range(TT):
                ts(yld[:, 0, t, :], x[:, t, :], rs[:, t:t + 1], None, ALU.mult)
                v.drain()
                tt(yld[:, 0, t, :], yld[:, 0, t, :], g_row[:, :], ALU.mult).then_inc(fin_ok, 1)

        @block.gpsimd
        def _(pool):
            g = nc.gpsimd
            for s, a, b in MASK_PARTS:
                pool.dma_start(mask_f32[:, a:b], masks[:, a:b]).then_inc(s, ahead[s])
            pool.sem_inc(mlo_ok, ahead[mlo_ok] + 1)
            with pool.Fori(0, L) as l:
                pool.wait_ge(x_ok, (l + 1) * TT)
                pool.dma_start(par[:, :], params[bass.ds(l, 1), :, :].rearrange("o p n -> p (o n)")).then_inc(par_ld, 16)
                for i, (b, kind, idx) in enumerate(QKV):
                    if kind == V:
                        continue
                    r = ROPES[i]
                    pool.wait_ge(pj_act, l * NQ + i + 1)
                    g.tensor_tensor(swp[:, r % 2, :], swp[:, r % 2, :], c(C_SIN, T), ALU.mult).then_inc(sn_ok, 1)
                    pool.wait_ge(sn_ok, l * ROPES[NQ] + r + 1)
                    need(pool, pj_dve, l * ROPES[NQ] + r + 1)
                    if b == 0:
                        g.tensor_tensor(qk_a[:, idx, :], rca[:, r % 2, :], swp[:, r % 2, :], ALU.add).then_inc(rope_ok, 1)
                    elif idx == 1:
                        g.tensor_tensor(qk_b[:, idx, :], rca[:, r % 2, :], swp[:, r % 2, :], ALU.add).then_inc(rope_ok, 1)
                    else:
                        g.tensor_tensor(in_order(qk_b[:, idx, :]), by_residue(rca[:, r % 2, :]), by_residue(swp[:, r % 2, :]),
                                        ALU.add).then_inc(rope_ok, 1)
                with pool.Fori(0, KD // 2) as it:
                    for half in range(2):
                        n = l * KD + it * 2 + half
                        need(pool, br_ok, n + 2)
                        g.tensor_tensor(mab[:, half, 0, :], mab[:, half, 0, :], mab[:, half, 1, :], ALU.add).then_inc(sum_ok, 1)
                        pool.wait_ge(mhi_ok, n + 1)
                        g.tensor_tensor(m_lo[:, bass.ds(it * 2 + half, 1), :].rearrange("p o n -> p (o n)"), mab[:, half, 0, :],
                                        m_hi[:, bass.ds(it * 2 + half, 1), :].bitcast(FP32).rearrange("p o n -> p (o n)"),
                                        ALU.subtract).then_inc(mlo_ok, 1)
                need(pool, mlo_ok, l * KD + KD + 1)
                pool.dma_start(g_row[:, :], g_rows[bass.ds(l, 1), :, :].rearrange("o p n -> p (o n)")).then_inc(gr_ld, 16)

                def scatter(s, done):
                    pool.indirect_dma_start(out=y_rows[:, :], out_offset=bass.IndirectOffsetOnAxis(ap=idx_row[:, s:s + 1].bitcast(U32), axis=0),
                                            in_=yb[:, s, :], in_offset=None, bounds_check=2 * T - 1, oob_is_err=False).then_inc(done, 16)

                with pool.Fori(0, PAIRS // 2) as it:
                    for s in range(2):
                        n = l * PAIRS + it * 2 + s
                        need(pool, ya_ok, n + 1)
                        hold(pool, yd_ok, n + 1 + ahead[yd_ok])
                        scatter(s, ysc[s])

                def more_experts(r, p, q):
                    hold(pool, ov_y, q + 1)
                    scatter(0, ov_sc)

                overflow(pool, l, more_experts)
            pool.wait_ge(x_ok, L * TT + 1)
            pool.dma_start(g_row[:, :], g_rows[L, :, :]).then_inc(gr_ld, 16)


def constants(np):
    inv = (1.0 / (np.float32(10000.0) ** (np.arange(0, DH, 2, dtype=np.float32) / np.float32(DH)))).astype(np.float32)
    ang = (np.arange(T, dtype=np.float32)[:, None] * inv[None, :]).astype(np.float32)
    cos, sin = np.cos(ang).T.astype(np.float32), np.sin(ang).T.astype(np.float32)
    k = np.zeros((P, C_END), np.float32)
    k[:, C_COS:C_COS + T] = np.concatenate([cos] * 4)
    k[:, C_SIN:C_SIN + T] = np.concatenate([-sin, sin] * 2)
    k[:, C_ID:C_ID + P] = np.eye(P)
    k[:, C_TRI:C_TRI + P] = np.triu(np.ones((P, P)), 1)
    k[:, C_ONE:C_ONE + P] = 1.0
    k[:, C_IOTA:C_IOTA + CAP] = np.arange(CAP)
    tok = np.arange(T).reshape(TT, P).T
    k[:, C_TOK:C_TOK + TT] = tok - BIG
    k[:, C_TOK + TT:C_TOK + 2 * TT] = tok + T - BIG
    k[:, C_THR:C_THR + 7] = CAP * np.arange(1, 8)
    q = np.arange(P)[:, None]
    off = -1e30
    ma = np.where(np.abs(np.arange(-P, 2 * P)[None, :] - q) <= 128, 0.0, off)
    place = np.arange(P)
    tokens = 16 * (place % 32) + 4 * (place // 32)
    mb = [np.where(np.abs(np.arange(T)[None, :] - (tokens + r)[:, None]) <= 64, 0.0, off) for r in range(4)]
    m1 = np.where(np.abs(tokens[None, :] // 4 - tokens[:, None] // 4) <= 64, 0.0, off)
    m2 = np.where(tokens[None, :] % 16 == tokens[:, None] % 16, 0.0, off)
    return k, np.concatenate([ma, *mb, m1, m2], axis=1).astype(np.float32)


def lay_out(np, w):
    w_in, L = w["w_in"], w["w_in"].shape[0]
    stream = np.zeros((L, NT, P, KD, P), np.float32)

    def tile(cols):
        return w_in[:, :, cols].reshape(L, KD, P, len(cols)).transpose(0, 2, 1, 3)

    ar = np.arange
    a_q = [np.concatenate([j * DH + ar(DH), (j + 4) * DH + ar(DH)]) for j in range(4)]
    for i, (b, kind, idx) in enumerate(QKV):
        if b == 0:
            cols = 640 + ar(P) if kind == V else 512 + ar(P) if idx == 4 else a_q[idx]
        else:
            pair = (b - 1) * P
            if kind == V:
                cols = 768 + idx * 768 + 512 + pair + ar(P)
            else:
                cols = 768 + (idx // 2) * 768 + (idx % 2) * 256 + pair + ar(P)
        stream[:, i] = tile(cols)
    rows_a = np.concatenate(a_q)
    wa = w["w_branch_a"][:, rows_a, :].reshape(L, 4, P, D)
    wb = w["w_branch_b"].reshape(L, 2, P, D)
    for m in range(KD):
        i = NQ + 3 * m
        cols = m * P + ar(P)
        stream[:, i] = tile(3072 + cols)
        stream[:, i + 1] = tile(4096 + cols)
        stream[:, i + 2, :, 0:4] = wa[..., cols].transpose(0, 2, 1, 3)
        stream[:, i + 2, :, 4:6] = wb[..., cols].transpose(0, 2, 1, 3)
    stream = stream.reshape(L, NT, P, D)
    wo = w["w_out"].reshape(L, 4, 2, P, 2, T)
    for dh in range(2):
        for kp in range(4):
            stream[:, NQ + NGATE + 4 * dh + kp] = wo[:, kp, :, :, dh].transpose(0, 2, 1, 3).reshape(L, P, D)

    def up(a):
        return a.reshape(L, NE, KD, P, FE).transpose(0, 1, 3, 2, 4)

    gu_w = np.concatenate([up(w["w_exp_gate"]), up(w["w_exp_up"])], axis=-1).reshape(L * PAIRS, 2, P, KD * 2 * FE)
    dn_w = w["w_exp_down"].reshape(L, NE, 2, P, D).transpose(0, 1, 3, 2, 4).reshape(L * PAIRS, 2, P, 2 * D)
    router = np.concatenate([w["w_router_group"], w["w_router_expert"]], axis=-1)
    router = router.reshape(L, KD, P, NLOG).transpose(0, 2, 1, 3).reshape(L, P, KD * NLOG)
    bias = np.concatenate([w["b_router_group"], w["b_router_expert"]], axis=-1)
    bias = np.broadcast_to(bias[:, None, :], (L, P, NLOG))
    g_col = w["attn_norm_g"].reshape(L, KD, P).transpose(0, 2, 1)
    order = [h for j in range(4) for h in (j, j + 4)]
    sink = np.broadcast_to(w["a_sink"][:, None, order], (L, P, 8))
    params = np.concatenate([router, bias, g_col, sink], axis=-1)
    g_rows = np.concatenate([w["ffn_norm_g"], w["final_norm_g"][None]])
    g_rows = np.broadcast_to(g_rows[:, None, :], (L + 1, P, D))
    return [np.ascontiguousarray(a) for a in (w["x"].reshape(T, D), stream, gu_w, dn_w, params, g_rows)]


def kernel(**inputs):
    import numpy as np
    import concourse.bacc as bacc
    from concourse.bass_utils import run_bass_kernel_spmd

    w = {k: np.asarray(v) for k, v in inputs.items()}
    names = ["x", "stream", "gu_w", "dn_w", "params", "g_rows", "consts", "masks"]
    arrays = dict(zip(names, [*lay_out(np, w), *constants(np)]))
    nc = bacc.Bacc("TRN2", target_bir_lowering=False, num_devices=1)
    args = [nc.dram_tensor(f"in_{n}", arrays[n].shape, FP32, kind="ExternalInput").ap() for n in names]
    args.append(nc.dram_tensor("out_x", (T, D), FP32, kind="ExternalOutput").ap())
    hybrid_encoder(nc, *args)
    r = run_bass_kernel_spmd(nc, [{f"in_{n}": arrays[n] for n in names}], core_ids=[0])
    return r.results[0]["out_x"].reshape(1, T, D)
```

```python
import math
from contextlib import ExitStack

import concourse.bass as bass
from concourse import mybir

FP32 = mybir.dt.float32
F32R = mybir.dt.float32r
BF16 = mybir.dt.bfloat16
I32 = mybir.dt.int32
U32 = mybir.dt.uint32
ALU = mybir.AluOpType
ACT = mybir.ActivationFunctionType
AX = mybir.AxisListType

P = 128
T = 512
TT = T // P
D = 1024
KD = D // P
DH = 64
EPS = 1e-6
SCALE = DH ** -0.5
NE = 32
NGRP = 4
EPG = NE // NGRP
FE = 256
CAP = 64
PAIRS = NE // 2
BIG = 4096.0
NEVER = 1000.0
NLOG = NGRP + NE
PARAMS = KD * NLOG + NLOG + 2 * KD + 8

V, R = "v", "rope"
BLOCK_A = [(V, 0), (R, 4), (R, 0), (R, 1), (R, 2), (R, 3)]
BLOCK_B = [(V, 0), (V, 1), (V, 2), (R, 0), (R, 1), (R, 2), (R, 3), (R, 4), (R, 5)]
BLOCKS = [BLOCK_A, BLOCK_B, BLOCK_B]
QKV = [(b, kind, idx) for b, blk in enumerate(BLOCKS) for kind, idx in blk]
NQ = len(QKV)
NGATE = 3 * KD
NOUT = 8
NT = NQ + NGATE + NOUT
ROPES = [sum(1 for q in QKV[:i] if q[1] == R) for i in range(NQ + 1)]
VS = [sum(1 for q in QKV[:i] if q[1] == V) for i in range(NQ + 1)]
SWAPS = [(ROPES[NQ] + 1) // 2, ROPES[NQ] // 2]
BLOCK_AT = [0, len(BLOCK_A), len(BLOCK_A) + len(BLOCK_B)]
NSTEP_A, NSTEP_B = 16, 4
STEPS = NSTEP_A + 2 * NSTEP_B
NEEDS = {0: 0, NSTEP_A: 1, NSTEP_A + NSTEP_B: 2}


def attention_order():
    order, turned = [], [0]
    for i in range(BLOCK_AT[1] + 1):
        order.append(("tile", i))
        if i == 1:
            order.append(("turn", 0))
    order += [("scores", 0), ("scores", 1)]
    waiting, nxt = [BLOCK_AT[1]], BLOCK_AT[1] + 1
    order += [("turn", waiting.pop()), ("tile", nxt)]
    if QKV[nxt][1] == V:
        waiting.append(nxt)
    nxt += 1
    for u in range(STEPS):
        order.append(("transpose", u))
        last = nxt
        if nxt < NQ:
            order.append(("tile", nxt))
            nxt += 1
        if waiting:
            order.append(("turn", waiting.pop(0)))
        if last < NQ and QKV[last][1] == V:
            waiting.append(last)
        if u + 2 < STEPS:
            order.append(("scores", u + 2))
        if u >= STEPS - 2:
            order.append(("gate", u - STEPS + 2))
        order.append(("values", u))
    assert nxt == NQ and not waiting
    return order


ORDER = attention_order()
K_ORDER = [6, 7, 0, 1, 2, 3, 4, 5]
C_COS, C_SIN, C_ID, C_TRI, C_ONE, C_IOTA = 0, 512, 1024, 1152, 1280, 1408
C_TOK = C_IOTA + CAP
C_THR = C_TOK + 8
C_END = C_THR + 8
MA, MB = 3 * P, T + 2 * P


def hybrid_encoder(nc, x_in, stream, gu_w, dn_w, params, g_rows, consts, masks, out):
    L = stream.shape[0]
    y_rows = nc.dram_tensor("y_rows", (2 * T, D), FP32, kind="Internal").ap()

    def at(name, offset, shape, dt):
        return nc.alloc_sbuf_tensor_at(name, [P, *shape], dt, offset=offset)

    def after(n):
        return -(-n // 32) * 32

    KB = 1024
    base = after(nc.sbuf_base)
    R_X, R_C, R_W, R_H, R_Q, R_S = (base + n * KB for n in (0, 16, 31, 79, 135, 183))
    x = at("x", R_X, [TT, D], FP32)
    cst = at("cst", R_C, [C_END], FP32)
    o = R_C + 4 * C_END
    mask_a = at("mask_a", o, [MA], BF16); o = after(o + 2 * MA)
    mask_b = at("mask_b", o, [TT, T], BF16); o = after(o + 2 * TT * T)
    mask_b12 = at("mask_b12", o, [2 * P], BF16); o = after(o + 4 * P)
    par = at("par", o, [PARAMS], FP32); o = after(o + 4 * PARAMS)
    wr = par[:, 0:KD * NLOG].rearrange("p (k n) -> p k n", n=NLOG)
    br = par[:, KD * NLOG:KD * NLOG + NLOG]
    g_col = par[:, KD * NLOG + NLOG:KD * NLOG + NLOG + KD]
    g2_col = par[:, KD * NLOG + NLOG + KD:KD * NLOG + NLOG + 2 * KD]
    sink = par[:, PARAMS - 8:PARAMS]
    nsink = at("nsink", o, [8], FP32); o = after(o + 32)
    small = at("small", o, [288], FP32); o = after(o + 4 * 288)
    gl8 = small[:, 96:128].rearrange("p (t n) -> p t n", n=8)
    cum = small[:, 128:288].rearrange("p (t n) -> p t n", n=NE)
    assert o <= R_W, o
    gu = [at("gu0", R_W, [2, KD, 2 * FE], FP32), at("gu1", R_H, [2, KD, 2 * FE], FP32)]
    dn = [at("dn0", R_W + 32 * KB, [2, 2, D], FP32), at("dn1", R_H + 32 * KB, [2, 2, D], FP32)]
    h_hi = at("h_hi", R_H, [KD, T], F32R)
    h_lo = at("h_lo", R_H + 16 * KB, [KD, T], F32R)
    o_hi = at("o_hi", R_H + 32 * KB, [6, T], F32R)
    o_lo = at("o_lo", R_H + 44 * KB, [6, T], F32R)
    qk_a = at("qk_a", R_Q, [5, T], FP32)
    v_a = at("v_a", R_Q + 10 * KB, [TT, P], FP32)
    qk_b = [at("qk_b0", R_Q + 12 * KB, [6, T], FP32), at("qk_b1", R_W, [6, T], FP32)]
    v_b = [at("v_b0", R_Q + 24 * KB, [3, TT, P], FP32), at("v_b1", R_W + 12 * KB, [3, TT, P], FP32)]
    vt = at("vt", R_W + 18 * KB, [2, T], FP32)
    swp = at("swp", R_W + 22 * KB, [2, T], FP32)
    rca = at("rca", R_W + 26 * KB, [2, T], FP32)
    pj = at("pj", R_W + 30 * KB, [2, T], FP32)
    prob = at("prob", R_Q + 30 * KB, [2, 2, MB], FP32)
    pt = at("pt", R_Q + 42 * KB, [2, MB], FP32)
    m_hi = at("m_hi", R_Q, [KD, T], F32R)
    m_lo = at("m_lo", R_Q + 16 * KB, [KD, T], F32R)
    sg = at("sg", R_Q + 32 * KB, [2, 2, T], FP32)
    mab = at("mab", R_Q + 40 * KB, [2, 2, T], FP32)
    xn = at("xn", R_Q, [TT, D], FP32)
    h2_hi = at("h2_hi", R_Q, [TT, D], F32R)
    h2_lo = at("h2_lo", R_Q + 16 * KB, [TT, D], F32R)
    yb = at("yb", R_Q + 32 * KB, [2, D], FP32)
    xn2 = yb
    junk = at("junk", R_Q + 44 * KB, [2, D], BF16)
    g_row = at("g_row", R_Q + 40 * KB, [D], FP32)
    sel = at("sel", R_Q + 40 * KB, [2, TT, P], F32R)
    z = at("z", R_Q + 44 * KB, [FE], FP32)
    zt = at("zt", R_Q + 45 * KB, [2, P], FP32)
    sil = at("sil", R_Q + 46 * KB, [FE], FP32)
    yld = at("yld", R_Q, [2, TT, D], FP32)
    raw = at("raw", R_S, [2, 1024], FP32)
    w_hi = [at(f"w_hi{i}", R_S + (8 + 8 * i) * KB, [1024], F32R) for i in range(2)]
    w_lo = [at(f"w_lo{i}", R_S + (12 + 8 * i) * KB, [1024], F32R) for i in range(2)]
    xtr = at("xtr", R_S + 8 * KB, [KD, T], FP32)
    xg = at("xg", R_S + 8 * KB, [D], FP32)
    xgt = at("xgt", R_S + 12 * KB, [KD, P], FP32)
    rt = at("rt", R_S + 16 * KB, [2048], FP32)
    mask_f32 = at("mask_f32", R_W, [MA + TT * T + 2 * P], FP32)

    def c(a, n):
        return cst[:, a:a + n]

    ident = c(C_ID, P)

    _w = [0]

    def word(n, *shape):
        a = _w[0]
        _w[0] += n
        v = rt[:, a:a + n]
        if len(shape) == 2:
            v = v.rearrange("p (a b) -> p a b", b=shape[1])
        if len(shape) == 3:
            v = v.rearrange("p (a b c) -> p a b c", b=shape[1], c=shape[2])
        return v

    rankm = word(TT * NE, TT, NE)
    info = word(TT * 2 * NE, TT, 2, NE)
    elog = word(TT * NE, TT, NE)
    lgt = word(T)
    lsc = word(TT * NLOG, TT, NLOG)
    top_g = word(TT * 8, TT, 8)
    idx_g = word(TT * 8, TT, 8)
    top_e = word(TT * 8, TT, 8)
    idx_e = word(TT * 8, TT, 8)
    idxf = word(TT * 3, TT, 3)
    oh_g = word(TT * NGRP, TT, NGRP)
    el8 = word(TT * 8, TT, 8)
    oh1 = word(TT * NE, TT, NGRP, EPG)
    oh2 = word(TT * NE, TT, NGRP, EPG)
    elm = oh1
    oh8 = word(TT * 2 * EPG, TT, 2, EPG)
    asg = word(TT * NE, TT, NE)
    rtmp = elog
    ge = word(TT * NGRP, TT, NGRP)
    wts = word(TT * 8, TT, 8)
    assert _w[0] <= 2048, _w[0]
    more = small[:, 40:48]
    rounds_f = small[:, 48:50]
    rounds_i = at("rounds_i", R_C + 15 * KB - 64, [2 * 4], I32)
    idx_row = at("idx_row", R_C + 15 * KB - 32, [2], I32)
    wslot = small[:, 52:54]
    ss, ms, rs = small[:, 0:4], small[:, 4:8], small[:, 8:12]
    nt1, nt2 = small[:, 12:16], small[:, 16:20]
    nmx, den, es = small[:, 20:24], small[:, 24:28], small[:, 28:32]
    nm2 = small[:, 32:36]
    rsum = small[:, 36:40]
    cnt_s = small[:, 56:64]
    spare = small[:, 64:65]

    ctx = ExitStack()
    with ctx:
        bank = [ctx.enter_context(nc.psum_tensor(f"bank{i}", [P, T], FP32)) for i in range(8)]

        def sem(name):
            return ctx.enter_context(nc.semaphore(name))

        def sems(*names):
            return [sem(n) for n in names]

        cst_ld, par_ld, gr_ld = sems("cst_ld", "par_ld", "gr_ld")
        x_ld = sems(*(f"x_ld{t}" for t in range(TT)))
        raw_ld = sems("raw_ld0", "raw_ld1")
        hi_ok, lo_ok, w_used = sems("hi_ok", "lo_ok", "w_used")
        x_ok, sq_ok, ms_ok, rt_ok, rs_ok, xn_ok, xt_ok = sems("x_ok", "sq_ok", "ms_ok", "rt_ok", "rs_ok", "xn_ok", "xt_ok")
        hhi_ok, hlo_ok = sems("hhi_ok", "hlo_ok")
        pj_act, pj_dve, sn_ok, rope_ok, vt_ok, v_ok = sems("pj_act", "pj_dve", "sn_ok", "rope_ok", "vt_ok", "v_ok")
        sw_ld = sems("sw_ld0", "sw_ld1")
        sc_ok, mx_ok, ex_ok, pr_ok, tr_ok = sems("sc_ok", "mx_ok", "ex_ok", "pr_ok", "tr_ok")
        pta_ok, ptd_ok, pv_ok, ohi_ok, olo_ok = sems("pta_ok", "ptd_ok", "pv_ok", "ohi_ok", "olo_ok")
        sig_ok, br_ok, sum_ok, mhi_ok, mlo_ok = sems("sig_ok", "br_ok", "sum_ok", "mhi_ok", "mlo_ok")
        om_ok, xo_ok = sems("om_ok", "xo_ok")
        xtr_ok, xtra_ok, xtrd_ok = sems("xtr_ok", "xtra_ok", "xtrd_ok")
        h2_ok, h2hi_ok, h2lo_ok = sems("h2_ok", "h2hi_ok", "h2lo_ok")
        lgt_ok, lgs_ok, lg_ok, rd_ok, ra_ok, rk_ok, lgd_ok, route_ok = sems(
            "lgt_ok", "lgs_ok", "lg_ok", "rd_ok", "ra_ok", "rk_ok", "lgd_ok", "route_ok")
        piece_ld = sem("piece_ld")
        gu_ld, dn_ld = sems("gu_ld0", "gu_ld1"), sems("dn_ld0", "dn_ld1")
        sel_ok, ga_ok, xga_ok, xgd_ok, xgt_ok, xta_ok, xtd_ok = sems(
            "sel_ok", "ga_ok", "xga_ok", "xgd_ok", "xgt_ok", "xta_ok", "xtd_ok")
        gu_ok, sil_ok, z_ok, zt_ok, zte_ok, dn_ok, ya_ok, yd_ok = sems(
            "gu_ok", "sil_ok", "z_ok", "zt_ok", "zte_ok", "dn_ok", "ya_ok", "yd_ok")
        inf_ok, ix_ok = sems("inf_ok", "ix_ok")
        ysc = sems("ysc0", "ysc1")
        yl_ld = [sems(*(f"yl_ld{k}_{t}" for t in range(TT))) for k in range(2)]
        fin_ok, out_st = sems("fin_ok", "out_st")
        ov_ld, ov_sel, ov_inf, ov_ga, ov_xg, ov_xt, ov_xe, ov_gu, ov_sil, ov_z, ov_zt, ov_ze, ov_dn, ov_y, ov_sc = sems(
            *("ov_" + n for n in ("ld", "sel", "inf", "ga", "xg", "xt", "xe", "gu", "sil", "z", "zt", "ze", "dn", "y", "sc")))

        ahead = {hi_ok: 1, lo_ok: 1, dn_ok: 1, z_ok: 1, ya_ok: 1, yd_ok: 1, sig_ok: 1, br_ok: 1, mlo_ok: 1, pv_ok: 1,
                 mx_ok: 1, ysc[0]: 16, ysc[1]: 16, ov_sc: 16}

        MASK_PARTS = ((ysc[0], 0, MA), (ysc[1], MA, MA + 2 * T), (ov_sc, MA + 2 * T, MA + TT * T + 2 * P))

        def need(eng, s, value):
            eng.wait_ge(s, value + ahead[s])

        held = {e.engine: sem(f"held_{n}") for n, e in
                (("sp", nc.sync), ("act", nc.scalar), ("pe", nc.tensor), ("dve", nc.vector), ("pool", nc.gpsimd))}

        block = ctx.enter_context(nc.Block())

        def by_residue(ap):
            return ap.rearrange("p (a c r) -> p r c a", c=4, r=4)

        def in_order(ap):
            return ap.rearrange("p (r c a) -> p r c a", r=4, c=4)

        def hold(eng, s, value):
            eng.wait_ge(s, value)
            eng.sem_inc(held[eng.engine], 1)

        def overflow(eng, l, body):
            hold(eng, route_ok, l + 1)
            extra = eng.value_load(rounds_i[0:1, bass.ds(2 * l, 1)], min_val=0, max_val=7)
            before = eng.value_load(rounds_i[0:1, bass.ds(2 * l + 1, 1)], min_val=0, max_val=7 * PAIRS * 2)
            with eng.If(extra > 0):
                with eng.Fori(0, extra) as r:
                    with eng.Fori(0, PAIRS) as p:
                        body(r, p, before + r * PAIRS + p)

        @block.sync
        def _(sp):
            for t in range(TT):
                sp.dma_start(x[:, t, :], x_in[t * P:(t + 1) * P, :]).then_inc(x_ld[t], 16)

            def load_tile(l, i):
                if i >= 2:
                    need(sp, hi_ok, l * NT + i - 1)
                    need(sp, lo_ok, l * NT + i - 1)
                else:
                    need(sp, hi_ok, l * NT)
                    need(sp, lo_ok, l * NT)
                sp.dma_start(raw[:, i % 2, :], stream[bass.ds(l, 1), i, :, :].rearrange("o p n -> p (o n)")).then_inc(raw_ld[i % 2], 16)

            def load_gu(l, p, s):
                sp.dma_start(gu[s][:, :, :, :].rearrange("p e k n -> p e (k n)"),
                             gu_w[bass.ds(l * PAIRS + p, 1), :, :, :].rearrange("o e p n -> p (o e) n")).then_inc(gu_ld[s], 16)

            def load_dn(l, p, s):
                sp.dma_start(dn[s][:, :, :, :].rearrange("p e k n -> p e (k n)"),
                             dn_w[bass.ds(l * PAIRS + p, 1), :, :, :].rearrange("o e p n -> p (o e) n")).then_inc(dn_ld[s], 16)

            def load_piece(l, n):
                if n < 8:
                    e, k = divmod(n, 4)
                    dst, src = gu[0][:, e, 2 * k:2 * k + 2, :].rearrange("p k n -> p (k n)"), gu_w[bass.ds(l * PAIRS, 1), e, :, k * D:(k + 1) * D]
                else:
                    e, f = divmod(n - 8, 2)
                    dst, src = dn[0][:, e, f, :], dn_w[bass.ds(l * PAIRS, 1), e, :, f * D:(f + 1) * D]
                done = {7: gu_ld[0], 11: dn_ld[0]}.get(n, piece_ld)
                sp.dma_start(dst, src.rearrange("o p n -> p (o n)")).then_inc(done, 16)

            def swap_halves(l, i):
                if QKV[i][1] == V:
                    return
                r = ROPES[i]
                hold(sp, pj_act, l * NQ + i + 1)
                if r >= 2:
                    sp.wait_ge(rope_ok, l * ROPES[NQ] + r - 1)
                for q in range(4):
                    sp.dma_start(swp[q * 32:q * 32 + 32, r % 2, :], pj[(q ^ 1) * 32:(q ^ 1) * 32 + 32, r % 2, :]).then_inc(sw_ld[r % 2], 16)

            with sp.Fori(0, L) as l:
                for i in range(NT):
                    if 4 <= i < NQ + 4:
                        swap_halves(l, i - 4)
                    load_tile(l, i)
                    if i == NQ + 3:
                        need(sp, pv_ok, (l + 1) * STEPS)
                    if NQ + 3 <= i < NQ + 3 + 12:
                        load_piece(l, i - NQ - 3)
                sp.wait_ge(w_used, l * NT + NQ + NGATE)
                load_gu(l, 1, 1)
                load_dn(l, 1, 1)
                with sp.Fori(1, PAIRS // 2) as it:
                    for s in range(2):
                        sp.wait_ge(gu_ok, l * PAIRS + 2 * it + s - 1)
                        load_gu(l, 2 * it + s, s)
                        need(sp, dn_ok, l * PAIRS + 2 * it + s - 1)
                        load_dn(l, 2 * it + s, s)


                def more_experts(r, p, q):
                    need(sp, dn_ok, (l + 1) * PAIRS)
                    need(sp, ov_sc, q * 16)
                    sp.dma_start(gu[0][:, :, :, :].rearrange("p e k n -> p e (k n)"),
                                 gu_w[bass.ds(l * PAIRS + p, 1), :, :, :].rearrange("o e p n -> p (o e) n")).then_inc(ov_ld, 16)
                    sp.dma_start(dn[0][:, :, :, :].rearrange("p e k n -> p e (k n)"),
                                 dn_w[bass.ds(l * PAIRS + p, 1), :, :, :].rearrange("o e p n -> p (o e) n")).then_inc(ov_ld, 16)

                overflow(sp, l, more_experts)
                total = sp.value_load(rounds_i[0:1, bass.ds(2 * l + 3, 1)], min_val=0, max_val=7 * PAIRS * 2)
                for s in range(2):
                    need(sp, ysc[s], (l + 1) * PAIRS * 8)
                need(sp, ov_sc, total * 16)
                for t in range(TT):
                    for k in range(2):
                        sp.dma_start(yld[:, k, t, :], y_rows[k * T + t * P:k * T + (t + 1) * P, :]).then_inc(yl_ld[k][t], 16)
            for t in range(TT):
                sp.wait_ge(fin_ok, t + 1)
                sp.dma_start(out[t * P:(t + 1) * P, :], yld[:, 1, t, :]).then_inc(out_st, 16)
            sp.wait_ge(out_st, TT * 16)

        def tile_bank(i):
            return 6 + i % 2 if i < BLOCK_AT[1] else 6

        BANK_BEFORE = {i: max(j for j in range(i) if tile_bank(j) == tile_bank(i)) for i in range(2, NQ)}

        @block.tensor
        def _(pe):
            mm = nc.tensor.matmul

            def three(dst, a, b, start, stop):
                (ah, al), (bh, bl) = a, b
                mm(dst, ah, bh, start=start, stop=False)
                mm(dst, ah, bl, start=False, stop=False)
                return mm(dst, al, bh, start=False, stop=stop)

            def wt(i, k, n=P):
                s = i % 2
                return w_hi[s][:, k * n:(k + 1) * n], w_lo[s][:, k * n:(k + 1) * n]

            def project(dst, i, k0=0, src=(h_hi, h_lo), kn=KD):
                for k in range(kn):
                    last = three(dst, wt(i, k0 + k), (src[0][:, k, :], src[1][:, k, :]), k == 0, k == kn - 1)
                return last

            def keep_busy(dst, times):
                for _ in range(times):
                    mm(dst, ident, c(C_COS, dst.shape[-1]), start=True, stop=True)

            for s in (dn_ok, pv_ok):
                pe.sem_inc(s, ahead[s])
            pe.wait_ge(cst_ld, 16)
            with pe.Fori(0, L) as l:
                for t in range(TT):
                    pe.wait_ge(xn_ok, l * TT + t + 1)
                    for k in range(KD):
                        last = nc.tensor.transpose(bank[k][:, t * P:(t + 1) * P], xn[:, t, k * P:(k + 1) * P], ident)
                    last.then_inc(xt_ok, 1)
                    if t < TT - 1:
                        keep_busy(bank[7][:, (TT - 1) * P:], 7)

                def qkv_tile(i, l=l):
                    need(pe, lo_ok, l * NT + i + 1)
                    if i >= 2:
                        before = BANK_BEFORE[i] + 1
                        pe.wait_ge(pj_act, l * NQ + before)
                    if i == 0:
                        for n, k in enumerate(K_ORDER):
                            pe.wait_ge(hlo_ok, l * KD + n + 1)
                            last = three(bank[tile_bank(i)][:, :], wt(i, k), (h_hi[:, k, :], h_lo[:, k, :]), n == 0, n == KD - 1)
                    else:
                        last = project(bank[tile_bank(i)][:, :], i)
                    last.then_inc(w_used, 1)

                def transpose_v(i, l=l):
                    n = VS[i]
                    pe.wait_ge(pj_act, l * NQ + i + 1)
                    if n:
                        pe.wait_ge(v_ok, l * VS[NQ] + n)
                    before = [w for w in ORDER[:ORDER.index(("turn", i))] if w[0] == "transpose"]
                    if before:
                        pe.wait_ge(ptd_ok, l * STEPS + len(before))
                    for t in range(TT):
                        last = nc.tensor.transpose(bank[5][:, t * P:(t + 1) * P], vt[:, n % 2, t * P:(t + 1) * P], ident)
                    last.then_inc(vt_ok, 1)

                def scores(u, l=l):
                    if u < NSTEP_A and u % TT == 0:
                        pe.wait_ge(rope_ok, l * ROPES[NQ] + 2 + u // TT)
                    elif u in NEEDS:
                        end = BLOCK_AT[NEEDS[u]] + len(BLOCKS[NEEDS[u]])
                        pe.wait_ge(rope_ok, l * ROPES[NQ] + ROPES[end])
                    need(pe, mx_ok, l * STEPS + max(0, u - 1 if u < NSTEP_A else u))
                    for h in range(2):
                        rows = slice(h * DH, (h + 1) * DH)
                        if u < NSTEP_A:
                            j, t = divmod(u, TT)
                            k0, k1 = max(0, t - 1), min(TT, t + 2)
                            last = mm(bank[2 * (u % 2) + h][:, 0:(k1 - k0) * P], qk_a[rows, j, t * P:(t + 1) * P],
                                      qk_a[rows, 4, k0 * P:k1 * P], start=True, stop=True)
                    if u >= NSTEP_A:
                        pair, r = divmod(u - NSTEP_A, TT)
                        qk = qk_b[pair]
                        cols = slice(r * P, (r + 1) * P)
                        for h in range(2):
                            rows = slice(h * DH, (h + 1) * DH)
                            mm(bank[2 * h][:, :], qk[rows, 0, cols], qk[rows, 1, :], start=True, stop=True)
                        for g in (1, 2):
                            for h in range(2):
                                rows = slice(h * DH, (h + 1) * DH)
                                last = mm(bank[2 * h + 1][:, (g - 1) * P:g * P], qk[rows, 2 * g, cols],
                                          qk[rows, 2 * g + 1, cols], start=True, stop=True)
                    last.then_inc(sc_ok, 1)

                def transposes(u, l=l):
                    pe.wait_ge(pr_ok, l * STEPS + u + 1)
                    s = u % 2
                    if u == NSTEP_A:
                        pe.wait_ge(pj_act, (l + 1) * NQ)
                    if u < NSTEP_A:
                        t = u % TT
                        n = min(TT, t + 2) - max(0, t - 1)
                        for h in range(2):
                            if h:
                                turned = sum(1 for what, i in ORDER[:ORDER.index(("transpose", u))] if what == "turn")
                                pe.wait_ge(v_ok, l * VS[NQ] + turned)
                            for k in range(n):
                                last = nc.tensor.transpose(bank[4 + h][:, k * P:(k + 1) * P], prob[:, s, h, k * P:(k + 1) * P], ident)
                    else:
                        for h in range(2):
                            for k in range(TT):
                                nc.tensor.transpose(bank[4 + h][:, k * P:(k + 1) * P], prob[:, s, h, k * P:(k + 1) * P], ident)
                        for h in range(2):
                            for k in range(2):
                                last = nc.tensor.transpose(bank[6][:, (2 * h + k) * P:(2 * h + k + 1) * P],
                                                           prob[:, s, h, T + k * P:T + (k + 1) * P], ident)
                    last.then_inc(tr_ok, 1)

                def values(u, l=l):
                    pe.wait_ge(pta_ok, l * STEPS + u + 1)
                    pe.wait_ge(ptd_ok, l * STEPS + u + 1)
                    t = u % TT
                    pair = u // TT
                    if u in NEEDS:
                        end = BLOCK_AT[NEEDS[u]] + len(BLOCKS[NEEDS[u]])
                        pe.wait_ge(v_ok, l * VS[NQ] + VS[end])
                    if t == 0 and pair:
                        pe.wait_ge(ohi_ok, l * 6 + pair)
                        pe.wait_ge(olo_ok, l * 6 + pair)
                    cols = slice(t * P, (t + 1) * P)
                    if u < NSTEP_A:
                        k0, k1 = max(0, t - 1), min(TT, t + 2)
                        terms = [(lambda h, k=k: v_a[:, k, h * DH:(h + 1) * DH], (k - k0) * P) for k in range(k0, k1)]
                    else:
                        vb = v_b[pair - 4]
                        terms = [(lambda h, k=k: vb[:, 0, k, h * DH:(h + 1) * DH], k * P) for k in range(TT)]
                        terms += [(lambda h, g=g: vb[:, g, t, h * DH:(h + 1) * DH], T + (g - 1) * P) for g in (1, 2)]
                    for n, (v, c0) in enumerate(terms):
                        for h in range(2):
                            last = mm(bank[7][h * DH:(h + 1) * DH, cols], v(h), pt[:, h, c0:c0 + P],
                                      start=n == 0, stop=n == len(terms) - 1)
                    last.then_inc(pv_ok, 1)

                def first_gate(g, l=l):
                    if g == 0:
                        need(pe, mx_ok, (l + 1) * STEPS)
                    need(pe, lo_ok, l * NT + NQ + g + 1)
                    project(bank[g][:, :], NQ + g).then_inc(w_used, 1)

                act_on = {"tile": qkv_tile, "turn": transpose_v, "scores": scores, "transpose": transposes, "values": values,
                          "gate": first_gate}
                for what, i in ORDER:
                    act_on[what](i)

                def gates(it, half, l=l):
                    b4, i0 = 4 * (half % 2), NQ + 3 * half
                    need(pe, sig_ok, l * 2 * KD + it * 4 + 2 * half)
                    need(pe, br_ok, l * KD + it * 2 + half)
                    for gte in range(2):
                        need(pe, lo_ok, l * NT + it * 6 + i0 + gte + 1)
                        project(bank[b4 + gte][:, :], i0 + gte).then_inc(w_used, 1)

                def branch(it, half, l=l):
                    b4, i0 = 4 * half, NQ + 3 * half
                    need(pe, lo_ok, l * NT + it * 6 + i0 + 3)
                    project(bank[b4 + 2][:, :], i0 + 2, 0, (o_hi, o_lo), 4)
                    for k in range(2):
                        last = three(bank[b4 + 3][:, :], wt(i0 + 2, 4 + k), (o_hi[:, 4 + k, :], o_lo[:, 4 + k, :]), k == 0, k == 1)
                    last.then_inc(w_used, 1)

                hold(pe, olo_ok, l * 6 + 6)
                with pe.Fori(0, KD // 2 - 1) as it:
                    branch(it, 0)
                    gates(it, 1)
                    branch(it, 1)
                    gates(it, 2)
                branch(KD // 2 - 1, 0)
                gates(KD // 2 - 1, 1)
                branch(KD // 2 - 1, 1)

                def router_logits(t, l=l):
                    pe.wait_ge(xtra_ok, l * TT + t + 1)
                    pe.wait_ge(xtrd_ok, l * TT + t + 1)
                    for k in range(KD):
                        last = mm(bank[4][0:NLOG, t * P:(t + 1) * P], wr[:, k, :], xtr[:, k, t * P:(t + 1) * P],
                                  start=k == 0, stop=k == KD - 1)
                    return last

                for dh in range(2):
                    need(pe, br_ok, l * KD + KD + dh)
                    for kp in range(4):
                        if dh == 0:
                            pe.wait_ge(mhi_ok, l * KD + 2 * kp + 2)
                            need(pe, mlo_ok, l * KD + 2 * kp + 3)
                        i = NQ + NGATE + dh * 4 + kp
                        need(pe, lo_ok, l * NT + i + 1)
                        for t in range(TT):
                            for kk in range(2):
                                k = 2 * kp + kk
                                wh, wl = wt(i, kk, 512)
                                tok = slice(t * P, (t + 1) * P)
                                last = three(bank[4 * dh + t][:, :], (m_hi[:, k, tok], m_lo[:, k, tok]), (wh, wl), k == 0, k == KD - 1)
                            if kp == 3 and t < TT - 1:
                                last.then_inc(om_ok, 1)
                        last.then_inc(w_used, 1)

                for t in range(TT):
                    pe.wait_ge(xo_ok, l * 2 * TT + TT + t + 1)
                    if t >= 2:
                        pe.wait_ge(xtra_ok, l * TT + t - 1)
                        pe.wait_ge(xtrd_ok, l * TT + t - 1)
                    for k in range(KD):
                        last = nc.tensor.transpose(bank[2 * (t % 2) + k // 4][:, (k % 4) * P:(k % 4 + 1) * P],
                                                   x[:, t, k * P:(k + 1) * P], ident)
                    last.then_inc(xtr_ok, 1)
                    if t:
                        router_logits(t - 1)
                router_logits(TT - 1).then_inc(lgt_ok, 1)
                hold(pe, lgs_ok, l + 1)
                for t in range(TT):
                    last = nc.tensor.transpose(bank[5][:, t * NLOG:(t + 1) * NLOG], lgt[0:NLOG, t * P:(t + 1) * P], ident[0:NLOG, 0:NLOG])
                last.then_inc(lg_ok, 1)
                keep_busy(bank[7][:, :], 7)
                pe.wait_ge(rk_ok, l + 1)
                mm(bank[6][:, 0:(TT + 1) * NE], c(C_ONE, P), cum[:, :, :], start=True, stop=False)
                mm(bank[6][:, 0:TT * NE], c(C_TRI, P), asg[:, :, :], start=False, stop=True).then_inc(lgd_ok, 1)
                keep_busy(bank[7][:, :], 2)

                def gather(s, e0, info_done, done):
                    read_info(s, e0, info_done)
                    gather_rows(s, done)

                def read_info(s, e0, info_done):
                    for t in range(TT):
                        last = mm(bank[5][:, 2 * P:2 * P + 4], sel[:, s, t, :].bitcast(FP32), info[:, t, :, bass.ds(e0, 2)],
                                  start=t == 0, stop=t == TT - 1)
                    last.then_inc(info_done, 1)

                def gather_rows(s, done):
                    for t in range(TT):
                        for half in range(2):
                            for n, part in enumerate((h2_hi, h2_lo)):
                                last = mm(bank[half][:, :], sel[:, s, t, :], part[:, t, half * T:(half + 1) * T],
                                          start=t == 0 and n == 0, stop=t == TT - 1 and n == 1)
                    last.then_inc(done, 1)

                def turn(done):
                    for k in range(KD):
                        last = nc.tensor.transpose(bank[2 + k // 4][:, (k % 4) * P:(k % 4 + 1) * P], xg[:, k * P:(k + 1) * P], ident)
                    last.then_inc(done, 1)

                def up(s, done):
                    for k in range(KD):
                        for e in range(2):
                            last = mm(bank[4][e * CAP:(e + 1) * CAP, :], xgt[:, k, e * CAP:(e + 1) * CAP], gu[s][:, e, k, :],
                                      start=k == 0, stop=k == KD - 1)
                    last.then_inc(done, 1)

                def turn_z(done):
                    for f in range(2):
                        last = nc.tensor.transpose(bank[5][:, f * P:(f + 1) * P], z[:, f * P:(f + 1) * P], ident)
                    last.then_inc(done, 1)

                def down(s, done):
                    for half in range(2):
                        for f in range(2):
                            for e in range(2):
                                last = mm(bank[6 + half][e * CAP:(e + 1) * CAP, :], zt[:, f, e * CAP:(e + 1) * CAP],
                                          dn[s][:, e, f, half * T:(half + 1) * T], start=f == 0, stop=f == 1)
                    last.then_inc(done, 1)

                n0 = l * PAIRS
                pe.wait_ge(piece_ld, (l + 1) * 10 * 16)
                pe.wait_ge(sel_ok, n0 + 1)
                pe.wait_ge(h2lo_ok, l * TT + TT)
                gather_rows(0, ga_ok)
                pe.wait_ge(route_ok, l + 1)
                read_info(0, 0, inf_ok)
                keep_busy(bank[7][:, :], 1)
                pe.wait_ge(xga_ok, n0 + 1)
                pe.wait_ge(xgd_ok, n0 + 1)
                turn(xgt_ok)
                keep_busy(bank[7][:, :], 1)

                def pair(it, s, last_pair=False):
                    n = n0 + 2 * it + s
                    pe.wait_ge(xta_ok, n + 1)
                    pe.wait_ge(xtd_ok, n + 1)
                    pe.wait_ge(gu_ld[s], (l * (PAIRS // 2) + it + 1) * 16)
                    need(pe, z_ok, n)
                    up(s, gu_ok)
                    if not last_pair:
                        pe.wait_ge(sel_ok, n + 2)
                        gather(1 - s, 2 * (2 * it + s + 1), inf_ok, ga_ok)
                    need(pe, z_ok, n + 1)
                    if not last_pair:
                        pe.wait_ge(ix_ok, n + 2)
                    turn_z(zt_ok)
                    if not last_pair:
                        pe.wait_ge(xga_ok, n + 2)
                        pe.wait_ge(xgd_ok, n + 2)
                        turn(xgt_ok)
                    pe.wait_ge(zte_ok, n + 1)
                    pe.wait_ge(dn_ld[s], (l * (PAIRS // 2) + it + 1) * 16)
                    need(pe, ya_ok, n)
                    need(pe, yd_ok, n)
                    down(s, dn_ok)

                with pe.Fori(0, PAIRS // 2 - 1) as it:
                    pair(it, 0)
                    pair(it, 1)
                pair(PAIRS // 2 - 1, 0)
                pair(PAIRS // 2 - 1, 1, True)


                def more_experts(r, p, q):
                    need(pe, ya_ok, n0 + PAIRS)
                    need(pe, yd_ok, n0 + PAIRS)
                    pe.wait_ge(ov_sel, q + 1)
                    gather(0, 2 * p, ov_inf, ov_ga)
                    pe.wait_ge(ov_xg, q + 1)
                    turn(ov_xt)
                    pe.wait_ge(ov_xe, q + 1)
                    pe.wait_ge(ov_ld, (q + 1) * 32)
                    up(0, ov_gu)
                    pe.wait_ge(ov_z, q + 1)
                    turn_z(ov_zt)
                    pe.wait_ge(ov_ze, q + 1)
                    down(0, ov_dn)
                    pe.wait_ge(ov_y, q + 1)

                overflow(pe, l, more_experts)

        @block.scalar
        def _(act):
            run = nc.scalar.activation
            act.dma_start(cst[:, :], consts).then_inc(cst_ld, 16)
            for s in (hi_ok, ya_ok):
                act.sem_inc(s, ahead[s])
            act.sem_inc(sig_ok, ahead[sig_ok] + 2)

            def split_hi(l, i, it=0):
                act.wait_ge(raw_ld[i % 2], (l * (NT // 2) + it * 3 + i // 2 + 1) * 16)
                if i >= 2:
                    act.wait_ge(w_used, l * NT + it * 6 + i - 1)
                run(w_hi[i % 2][:, :], raw[:, i % 2, :], ACT.Copy).then_inc(hi_ok, 1)

            def square(t, l):
                act.wait_ge(x_ok, l * TT + t + 1)
                run(xn[:, t, :], x[:, t, :], ACT.Square, accum_out=ss[:, t:t + 1]).then_inc(sq_ok, 1)

            def root(t, n):
                act.wait_ge(ms_ok, n + 1)
                run(rs[:, t:t + 1], ms[:, t:t + 1], ACT.Sqrt).then_inc(rt_ok, 1)

            def scale_x(t, l):
                act.wait_ge(rs_ok, l * TT + t + 1)
                run(xn[:, t, :], x[:, t, :], ACT.Identity, scale=rs[:, t:t + 1]).then_inc(xn_ok, 1)

            def norm(l):
                for t in range(TT - 1):
                    square(t, l)
                    if t:
                        scale_x(t - 1, l)
                    root(t, 2 * l * TT + t)

            def load_table():
                run(spare, ms[:, 0:1], ACT.Sqrt)

            norm(0)
            with act.Fori(0, L) as l:
                square(TT - 1, l)
                scale_x(TT - 2, l)
                root(TT - 1, 2 * l * TT + TT - 1)
                split_hi(l, 0)
                scale_x(TT - 1, l)
                split_hi(l, 1)
                act.wait_ge(par_ld, (l + 1) * 16)
                act.wait_ge(xt_ok, l * TT + TT)
                for k in K_ORDER:
                    run(h_hi[:, k, :], bank[k][:, :], ACT.Identity, scale=g_col[:, k:k + 1]).then_inc(hhi_ok, 1)

                def epilogue(i, l=l):
                    _b, kind, idx = QKV[i]
                    act.wait_ge(w_used, l * NT + i + 1)
                    src = bank[tile_bank(i)]
                    if kind == V:
                        n = VS[i]
                        if n >= 2:
                            act.wait_ge(vt_ok, l * VS[NQ] + n - 1)
                        if _b and idx:
                            run(in_order(vt[:, n % 2, :]), by_residue(src[:, :]), ACT.Copy).then_inc(pj_act, 1)
                        else:
                            run(vt[:, n % 2, :], src[:, :], ACT.Copy).then_inc(pj_act, 1)
                        return
                    r = ROPES[i]
                    if r >= 2:
                        act.wait_ge(pj_dve, l * ROPES[NQ] + r - 1)
                        act.wait_ge(sw_ld[r % 2], (l * SWAPS[r % 2] + r // 2) * 64)
                    run(pj[:, r % 2, :], src[:, :], ACT.Copy).then_inc(pj_act, 1)

                def width(u):
                    t = u % TT
                    return (min(TT, t + 2) - max(0, t - 1)) * P if u < NSTEP_A else MB

                def exps(u, l=l):
                    need(act, mx_ok, l * STEPS + u + 1)
                    s = u % 2
                    if u < NSTEP_A:
                        run(es[:, 2 * s:2 * s + 2], nm2[:, 2 * s:2 * s + 2], ACT.Exp)
                    for h in range(2):
                        p = prob[:, s, h, 0:width(u)]
                        last = run(p, p, ACT.Exp, bias=nmx[:, 2 * s + h:2 * s + h + 1], scale=-1.0,
                                   accum_out=rsum[:, 2 * s + h:2 * s + h + 1])
                    last.then_inc(ex_ok, 1)

                def copy_pt(u, l=l):
                    act.wait_ge(tr_ok, l * STEPS + u + 1)
                    need(act, pv_ok, l * STEPS + u)
                    if u < NSTEP_A:
                        run(pt[:, 0, 0:width(u)], bank[4][:, 0:width(u)], ACT.Copy).then_inc(pta_ok, 1)
                    else:
                        run(pt[:, 0, 0:T], bank[4][:, :], ACT.Copy)
                        run(pt[:, :, T:MB], bank[6][:, :].rearrange("p (h n) -> p h n", h=2), ACT.Copy).then_inc(pta_ok, 1)

                def copy_o(pair, l=l):
                    need(act, pv_ok, l * STEPS + 4 * pair + 4)
                    if pair < 4:
                        run(o_hi[:, pair, :], bank[7][:, :], ACT.Copy).then_inc(ohi_ok, 1)
                    else:
                        run(by_residue(o_hi[:, pair, :]), in_order(bank[7][:, :]), ACT.Copy).then_inc(ohi_ok, 1)

                for what, i in ORDER:
                    if what == "tile":
                        if i:
                            split_hi(l, i + 1)
                        epilogue(i)
                    elif what == "scores":
                        exps(i)
                    elif what == "transpose":
                        copy_pt(i)
                    elif what == "gate":
                        split_hi(l, NQ + 1 + i)
                    elif what == "values" and i % TT == TT - 1:
                        copy_o(i // TT)

                with act.Fori(0, KD // 2) as it:
                    for half in range(2):
                        i0 = NQ + 3 * half
                        for gte in range(2):
                            act.wait_ge(w_used, l * NT + it * 6 + i0 + gte + 1)
                            if gte == 0:
                                need(act, br_ok, l * KD + it * 2 + half)
                            run(sg[:, half, gte, :], bank[4 * half + gte][:, :], ACT.Sigmoid).then_inc(sig_ok, 1)
                        split_hi(l, i0 + 3, it)
                        split_hi(l, i0 + 4, it)
                        act.wait_ge(sum_ok, l * KD + it * 2 + half + 1)
                        run(m_hi[:, bass.ds(it * 2 + half, 1), :].rearrange("p o n -> p (o n)"), mab[:, half, 0, :], ACT.Copy).then_inc(mhi_ok, 1)
                        split_hi(l, i0 + 5, it)
                for i in range(NQ + NGATE + 3, NT):
                    split_hi(l, i)
                load_table()

                for t in range(TT):
                    act.wait_ge(xo_ok, l * 2 * TT + TT + t + 1)
                    run(junk[:, t % 2, :], x[:, t, :], ACT.Square, accum_out=ss[:, t:t + 1]).then_inc(sq_ok, 1)
                for t in range(TT - 1):
                    root(t, (2 * l + 1) * TT + t)

                def copy_xtr(t, l=l):
                    act.wait_ge(xtr_ok, l * TT + t + 1)
                    run(xtr[:, 0:4, t * P:(t + 1) * P], bank[2 * (t % 2)][:, :].rearrange("p (k n) -> p k n", k=4),
                        ACT.Copy).then_inc(xtra_ok, 1)

                copy_xtr(0)
                root(TT - 1, (2 * l + 1) * TT + TT - 1)
                copy_xtr(1)
                for t in range(TT):
                    if t == TT - 1:
                        act.wait_ge(lgt_ok, l + 1)
                        run(lgt[0:NLOG, :], bank[4][0:NLOG, :], ACT.Copy).then_inc(lgs_ok, 1)
                    act.wait_ge(h2_ok, l * TT + t + 1)
                    run(h2_hi[:, t, :], xn2[:, t % 2, :], ACT.Copy).then_inc(h2hi_ok, 1)
                    if t + 2 < TT:
                        copy_xtr(t + 2)
                act.wait_ge(rd_ok, 2 * l + 1)
                run(ge, ge, ACT.Exp).then_inc(ra_ok, 1)
                act.wait_ge(rd_ok, 2 * l + 2)
                run(wts[:, :, 3:4], wts[:, :, 2:3], ACT.Exp).then_inc(ra_ok, 1)

                n0 = l * PAIRS

                def first_half(n):
                    act.wait_ge(ga_ok, n + 1)
                    run(xg[:, 0:T], bank[0][:, :], ACT.Copy).then_inc(xga_ok, 1)

                def turned(n):
                    act.wait_ge(xgt_ok, n + 1)
                    run(xgt[:, 0:4, :], bank[2][:, :].rearrange("p (k n) -> p k n", k=4), ACT.Copy).then_inc(xta_ok, 1)

                def pair(it, s, last_pair=False):
                    n = n0 + 2 * it + s
                    act.wait_ge(gu_ok, n + 1)
                    run(sil[:, :], bank[4][:, 0:FE], ACT.Silu).then_inc(sil_ok, 1)
                    if not last_pair:
                        first_half(n + 1)
                    act.wait_ge(zt_ok, n + 1)
                    need(act, dn_ok, n)
                    run(zt[:, :, :], bank[5][:, 0:FE].rearrange("p (f n) -> p f n", f=2), ACT.Copy).then_inc(zte_ok, 1)
                    if not last_pair:
                        turned(n + 1)
                    need(act, dn_ok, n + 1)
                    act.wait_ge(ix_ok, n + 1)
                    need(act, ysc[s], (l * (PAIRS // 2) + it) * 16)
                    run(yb[:, s, 0:T], bank[6][:, :], ACT.Identity, scale=wslot[:, s:s + 1]).then_inc(ya_ok, 1)

                first_half(n0)
                turned(n0)
                with act.Fori(0, PAIRS // 2 - 1) as it:
                    pair(it, 0)
                    pair(it, 1)
                pair(PAIRS // 2 - 1, 0)
                pair(PAIRS // 2 - 1, 1, True)

                def more_experts(r, p, q):
                    act.wait_ge(ov_gu, q + 1)
                    run(sil[:, :], bank[4][:, 0:FE], ACT.Silu).then_inc(ov_sil, 1)

                overflow(act, l, more_experts)
                load_table()
                norm(l + 1)
            square(TT - 1, L)
            scale_x(TT - 2, L)
            root(TT - 1, 2 * L * TT + TT - 1)
            scale_x(TT - 1, L)

        @block.vector
        def _(dve):
            v = nc.vector
            tt, ts, stt = v.tensor_tensor, v.tensor_scalar, v.scalar_tensor_tensor
            def masks_in():
                for s, _a, _b in MASK_PARTS:
                    dve.wait_ge(s, ahead[s])
                v.tensor_copy(mask_a[:, :], mask_f32[:, 0:MA])
                v.tensor_copy(mask_b[:, :, :], mask_f32[:, MA:MA + TT * T].rearrange("p (r n) -> p r n", n=T))
                v.tensor_copy(mask_b12[:, :], mask_f32[:, MA + TT * T:MA + TT * T + 2 * P])

            dve.wait_ge(cst_ld, 16)
            v.memset(rounds_i[0:1, :], 0)
            v.memset(gl8, -3.0e38)
            v.memset(cum[:, 0:1, :], 0.0)
            v.memset(rounds_f[:, :], 0.0)
            for s in (lo_ok, z_ok, yd_ok, mx_ok):
                dve.sem_inc(s, ahead[s])
            dve.sem_inc(br_ok, ahead[br_ok] + 1)
            v.drain()

            def split_lo(l, i, it=0):
                need(dve, hi_ok, l * NT + it * 6 + i + 1)
                tt(w_lo[i % 2][:, :], raw[:, i % 2, :], w_hi[i % 2][:, :].bitcast(FP32), ALU.subtract).then_inc(lo_ok, 1)

            def mean(t, n):
                one = slice(t, t + 1)
                dve.wait_ge(sq_ok, n + 1)
                ts(ms[:, one], ss[:, one], 1.0 / D, EPS, ALU.mult, ALU.add).then_inc(ms_ok, 1)

            def rstd(one, n):
                dve.wait_ge(rt_ok, n + 1)
                v.reciprocal(nt1[:, one], rs[:, one])
                v.drain()
                for t in range(one.start, one.stop):
                    t = slice(t, t + 1)
                    stt(nt2[:, t], nt1[:, t], nt1[:, t], ms[:, t], ALU.mult, ALU.mult)
                v.drain()
                ts(nt2[:, one], nt2[:, one], -0.5, 1.5, ALU.mult, ALU.add)
                v.drain()
                return tt(rs[:, one], nt1[:, one], nt2[:, one], ALU.mult)

            def h2_tile(t, l):
                if t >= 2:
                    dve.wait_ge(h2lo_ok, l * TT + t - 1)
                stt(xn2[:, t % 2, :], x[:, t, :], rs[:, t:t + 1], g_row[:, :], ALU.mult, ALU.mult).then_inc(h2_ok, 1)

            for t in range(TT):
                dve.wait_ge(x_ld[t], 16)
                dve.sem_inc(x_ok, 1)
                if t:
                    mean(t - 1, t - 1)
                    rstd(slice(t - 1, t), t - 1).then_inc(rs_ok, 1)
            masks_in()
            v.drain()
            with dve.Fori(0, L) as l:
                mean(TT - 1, 2 * l * TT + TT - 1)
                rstd(slice(TT - 1, TT), 2 * l * TT + TT - 1).then_inc(rs_ok, 1)
                split_lo(l, 0)
                split_lo(l, 1)
                for n, k in enumerate(K_ORDER):
                    dve.wait_ge(hhi_ok, l * KD + n + 1)
                    stt(h_lo[:, k, :], bank[k][:, :], g_col[:, k:k + 1], h_hi[:, k, :].bitcast(FP32), ALU.mult,
                        ALU.subtract).then_inc(hlo_ok, 1)

                def epilogue(i, l=l):
                    b, kind, idx = QKV[i]
                    if kind == V:
                        return
                    r = ROPES[i]
                    dve.wait_ge(pj_act, l * NQ + i + 1)
                    if r >= 2:
                        dve.wait_ge(rope_ok, l * ROPES[NQ] + r - 1)
                    tt(rca[:, r % 2, :], pj[:, r % 2, :], c(C_COS, T), ALU.mult).then_inc(pj_dve, 1)

                def copy_v(i, l=l):
                    b, kind, idx = QKV[i]
                    n = VS[i]
                    dve.wait_ge(vt_ok, l * VS[NQ] + n + 1)
                    dst = v_b[b - 1][:, idx, :, :] if b else v_a[:, :, :]
                    v.tensor_copy(dst, bank[5][:, :].rearrange("p (t n) -> p t n", t=TT)).then_inc(v_ok, 1)

                def maxima(u, l=l):
                    hold(dve, sc_ok, l * STEPS + u + 1)
                    s = u % 2
                    for h in range(2):
                        m = nmx[:, 2 * s + h:2 * s + h + 1]
                        if u < NSTEP_A:
                            j, t = divmod(u, TT)
                            k0, k1 = max(0, t - 1), min(TT, t + 2)
                            n = (k1 - k0) * P
                            c0 = (k0 - t + 1) * P
                            v.tensor_tensor_reduce(out=prob[:, s, h, 0:n], in0=bank[2 * (u % 2) + h][:, 0:n], in1=mask_a[:, c0:c0 + n],
                                                   scale=-SCALE, scalar=nsink[:, 2 * j + h:2 * j + h + 1], op0=ALU.add, op1=ALU.min, accum_out=m)
                        else:
                            r = (u - NSTEP_A) % TT
                            v.tensor_tensor_reduce(out=prob[:, s, h, 0:T], in0=bank[2 * h][:, :], in1=mask_b[:, r, :],
                                                   scale=-SCALE, scalar=3.0e38, op0=ALU.add, op1=ALU.min, accum_out=m)
                            v.tensor_tensor_reduce(out=prob[:, s, h, T:MB], in0=bank[2 * h + 1][:, 0:2 * P], in1=mask_b12[:, :],
                                                   scale=-SCALE, scalar=3.0e38, op0=ALU.add, op1=ALU.min,
                                                   accum_out=nm2[:, 2 * s + h:2 * s + h + 1])
                    v.drain()
                    two = slice(2 * s, 2 * s + 2)
                    if u < NSTEP_A:
                        tt(nm2[:, two], nmx[:, two], sink[:, 2 * j:2 * j + 2], ALU.add).then_inc(mx_ok, 1)
                    else:
                        tt(nmx[:, two], nmx[:, two], nm2[:, two], ALU.min).then_inc(mx_ok, 1)

                def normalise(u, l=l):
                    dve.wait_ge(ex_ok, l * STEPS + u + 1)
                    s = u % 2
                    two = slice(2 * s, 2 * s + 2)
                    if u < NSTEP_A:
                        t = u % TT
                        n = (min(TT, t + 2) - max(0, t - 1)) * P
                        tt(den[:, two], rsum[:, two], es[:, two], ALU.add)
                        v.drain()
                        v.reciprocal(den[:, two], den[:, two])
                    else:
                        n = MB
                        v.reciprocal(den[:, two], rsum[:, two])
                    v.drain()
                    for h in range(2):
                        p = prob[:, s, h, 0:n]
                        last = ts(p, p, den[:, 2 * s + h:2 * s + h + 1], None, ALU.mult)
                    last.then_inc(pr_ok, 1)

                def copy_pt(u, l=l):
                    dve.wait_ge(tr_ok, l * STEPS + u + 1)
                    need(dve, pv_ok, l * STEPS + u)
                    t = u % TT
                    n = (min(TT, t + 2) - max(0, t - 1)) * P if u < NSTEP_A else T
                    v.tensor_copy(pt[:, 1, 0:n], bank[5][:, 0:n]).then_inc(ptd_ok, 1)

                def copy_o(pair, l=l):
                    dve.wait_ge(ohi_ok, l * 6 + pair + 1)
                    hi, lo, src = o_hi[:, pair, :].bitcast(FP32), o_lo[:, pair, :], bank[7][:, :]
                    if pair >= 4:
                        hi, lo, src = by_residue(hi), by_residue(lo), in_order(src)
                    tt(lo, src, hi, ALU.subtract).then_inc(olo_ok, 1)

                dve.wait_ge(par_ld, (l + 1) * 16)
                ts(nsink[:, :], sink, -1.0, None, ALU.mult)
                tt(wr, wr, g2_col.rearrange("p (k o) -> p k o", o=1).to_broadcast([P, KD, NLOG]), ALU.mult)
                for what, i in ORDER:
                    if what == "tile":
                        if i:
                            split_lo(l, i + 1)
                        epilogue(i)
                    elif what == "turn":
                        copy_v(i)
                    elif what == "scores":
                        maxima(i)
                        if i == 1:
                            normalise(0)
                    elif what == "transpose":
                        copy_pt(i)
                        if i + 1 < STEPS:
                            normalise(i + 1)
                    elif what == "gate":
                        split_lo(l, NQ + 1 + i)
                    elif i % TT == TT - 1:
                        copy_o(i // TT)

                with dve.Fori(0, KD // 2) as it:
                    for half in range(2):
                        i0 = NQ + 3 * half
                        split_lo(l, i0 + 3, it)
                        need(dve, sig_ok, l * 2 * KD + it * 4 + 2 * half + 4)
                        dve.wait_ge(w_used, l * NT + it * 6 + i0 + 3)
                        need(dve, mlo_ok, l * KD + it * 2 + half)
                        tt(mab[:, half, 0, :], bank[4 * half + 2][:, :], sg[:, half, 0, :], ALU.mult)
                        tt(mab[:, half, 1, :], bank[4 * half + 3][:, :], sg[:, half, 1, :], ALU.mult).then_inc(br_ok, 1)
                        split_lo(l, i0 + 4, it)
                        split_lo(l, i0 + 5, it)
                for i in range(NQ + NGATE + 3, NT):
                    split_lo(l, i)
                    if i == NQ + NGATE + 5:
                        dve.wait_ge(w_used, l * NT + NQ + NGATE + 4)
                        for t in range(TT):
                            tt(x[:, t, 0:T], x[:, t, 0:T], bank[t][:, :], ALU.add).then_inc(xo_ok, 1)
                dve.wait_ge(gr_ld, (l + 1) * 16)

                def copy_xtr(t, l=l):
                    dve.wait_ge(xtr_ok, l * TT + t + 1)
                    v.tensor_copy(xtr[:, 4:8, t * P:(t + 1) * P], bank[2 * (t % 2) + 1][:, :].rearrange("p (k n) -> p k n", k=4)).then_inc(xtrd_ok, 1)

                for t in range(TT):
                    if t < TT - 1:
                        dve.wait_ge(om_ok, l * 6 + 4 + t)
                    else:
                        dve.wait_ge(w_used, l * NT + NT)
                    tt(x[:, t, T:D], x[:, t, T:D], bank[4 + t][:, :], ALU.add).then_inc(xo_ok, 1)
                    if t:
                        mean(t - 1, (2 * l + 1) * TT + t - 1)
                copy_xtr(0)
                mean(TT - 1, (2 * l + 1) * TT + TT - 1)
                copy_xtr(1)
                rstd(slice(0, TT), (2 * l + 1) * TT + TT - 1)
                v.drain()
                for t in range(TT):
                    h2_tile(t, l)
                    if t + 2 < TT:
                        copy_xtr(t + 2)

                dve.wait_ge(lg_ok, l + 1)
                logit = bank[5][:, 0:TT * NLOG].rearrange("p (t n) -> p t n", n=NLOG)

                def spread(ap, n):
                    return ap.rearrange("p (o n) -> p o n", o=1).to_broadcast([P, TT, n])

                tt(lsc, logit, rs.rearrange("p (t o) -> p t o", o=1).to_broadcast([P, TT, NLOG]), ALU.mult)
                v.drain()
                tt(gl8[:, :, 0:NGRP], lsc[:, :, 0:NGRP], spread(br[:, 0:NGRP], NGRP), ALU.add)
                tt(elog, lsc[:, :, NGRP:NLOG], spread(br[:, NGRP:NLOG], NE), ALU.add)
                v.drain()
                for t in range(TT):
                    v.max(top_g[:, t, :], gl8[:, t, :])
                v.drain()
                for t in range(TT):
                    v.max_index(idx_g[:, t, :].bitcast(U32), top_g[:, t, :], gl8[:, t, :])
                tt(ge, gl8[:, :, 0:NGRP], top_g[:, :, 0:1].to_broadcast([P, TT, NGRP]), ALU.subtract).then_inc(rd_ok, 1)
                v.drain()
                v.tensor_copy(idxf[:, :, 0:1], idx_g[:, :, 0:1].bitcast(U32))
                v.drain()
                tt(oh_g, spread(c(C_IOTA, NGRP), NGRP), idxf[:, :, 0:1].to_broadcast([P, TT, NGRP]), ALU.is_equal)
                v.drain()
                group = oh_g.rearrange("p t (g o) -> p t g o", o=1).to_broadcast([P, TT, NGRP, EPG])
                tt(elm, elog.rearrange("p t (g e) -> p t g e", e=EPG), group, ALU.mult)
                v.drain()
                v.tensor_reduce(el8, elm.rearrange("p t g e -> p t e g"), AX.X, ALU.add)
                v.drain()
                for t in range(TT):
                    v.max(top_e[:, t, :], el8[:, t, :])
                v.drain()
                for t in range(TT):
                    v.max_index(idx_e[:, t, :].bitcast(U32), top_e[:, t, :], el8[:, t, :])
                tt(wts[:, :, 2:3], top_e[:, :, 1:2], top_e[:, :, 0:1], ALU.subtract).then_inc(rd_ok, 1)
                v.drain()
                v.tensor_copy(idxf[:, :, 1:3], idx_e[:, :, 0:2].bitcast(U32))
                v.drain()
                for k in range(2):
                    tt(oh8[:, :, k, :], spread(c(C_IOTA, EPG), EPG), idxf[:, :, 1 + k:2 + k].to_broadcast([P, TT, EPG]), ALU.is_equal)
                v.drain()
                for k, dst in ((0, oh1), (1, oh2)):
                    tt(dst, group, oh8[:, :, k:k + 1, :].to_broadcast([P, TT, NGRP, EPG]), ALU.mult)
                v.drain()
                one = oh1.rearrange("p t g e -> p t (g e)")
                two_ = oh2.rearrange("p t g e -> p t (g e)")
                tt(asg, one, two_, ALU.add)
                v.drain()
                v.tensor_copy(cum[:, 1, :], asg[:, 0, :])
                tt(cum[:, 2, :], asg[:, 0, :], asg[:, 1, :], ALU.add)
                v.drain()
                tt(cum[:, 3, :], cum[:, 2, :], asg[:, 2, :], ALU.add)
                v.drain()
                tt(cum[:, 4, :], cum[:, 3, :], asg[:, 3, :], ALU.add).then_inc(rk_ok, 1)
                dve.wait_ge(ra_ok, 2 * l + 2)
                v.tensor_reduce(wts[:, :, 0], ge, AX.X, ALU.add)
                ts(wts[:, :, 4:5], wts[:, :, 3:4], 1.0, None, ALU.add)
                v.drain()
                v.reciprocal(wts[:, :, 1:2], wts[:, :, 0:1])
                v.reciprocal(wts[:, :, 5:6], wts[:, :, 4:5])
                v.drain()
                tt(wts[:, :, 6:7], wts[:, :, 1:2], wts[:, :, 5:6], ALU.mult)
                dve.wait_ge(lgd_ok, l + 1)
                stt(rankm, asg, NEVER, bank[6][:, 0:TT * NE].rearrange("p (t n) -> p t n", n=NE), ALU.mult, ALU.add)
                v.tensor_reduce(cnt_s[:, 0:1], bank[6][:, TT * NE:(TT + 1) * NE], AX.X, ALU.max)
                v.drain()
                ts(rankm, rankm, -NEVER, None, ALU.add)
                tt(wts[:, :, 7:8], wts[:, :, 6:7], wts[:, :, 3:4], ALU.mult)
                v.drain()

                n0 = l * PAIRS

                def choose(s, e0, done, shift=None):
                    src = rankm[:, :, bass.ds(e0, 2)]
                    for t in range(TT):
                        last = tt(sel[:, s, t, :].rearrange("p (e n) -> p e n", e=2),
                                  c(C_IOTA, CAP).rearrange("p (o n) -> p o n", o=1).to_broadcast([P, 2, CAP]),
                                  src[:, t, :].rearrange("p (e o) -> p e o", o=1).to_broadcast([P, 2, CAP]), ALU.is_equal)
                    last.then_inc(done, 1)

                def slots(s):
                    at0 = 2 * P
                    for e in range(2):
                        rows = slice(e * CAP, (e + 1) * CAP)
                        v.tensor_copy(wslot[rows, s:s + 1], bank[5][rows, at0 + e:at0 + e + 1])
                        last = ts(idx_row[rows, s:s + 1], bank[5][rows, at0 + 2 + e:at0 + 3 + e], BIG, None, ALU.add)
                    return last

                def second_half(n, s):
                    dve.wait_ge(ga_ok, n + 1)
                    v.tensor_copy(xg[:, T:D], bank[1][:, :]).then_inc(xgd_ok, 1)

                def turned(n):
                    dve.wait_ge(xgt_ok, n + 1)
                    v.tensor_copy(xgt[:, 4:8, :], bank[3][:, :].rearrange("p (k n) -> p k n", k=4)).then_inc(xtd_ok, 1)

                def pair(it, s, left=2):
                    n = n0 + 2 * it + s
                    dve.wait_ge(sil_ok, n + 1)
                    tt(z[:, :], bank[4][:, FE:2 * FE], sil[:, :], ALU.mult).then_inc(z_ok, 1)
                    if left >= 1:
                        dve.wait_ge(inf_ok, n + 2)
                        need(dve, ysc[1 - s], (l * (PAIRS // 2) + it + s) * 16)
                        slots(1 - s).then_inc(ix_ok, 1)
                        second_half(n + 1, 1 - s)
                        turned(n + 1)
                    if left >= 2:
                        choose(s, 2 * (2 * it + s + 2), sel_ok)
                    need(dve, dn_ok, n + 1)
                    need(dve, ysc[s], (l * (PAIRS // 2) + it) * 16)
                    ts(yb[:, s, T:D], bank[7][:, :], wslot[:, s:s + 1], None, ALU.mult).then_inc(yd_ok, 1)

                choose(0, 0, sel_ok)
                choose(1, 2, sel_ok)
                tok = c(C_TOK, 8)
                for which, (a1, a2) in enumerate(((wts[:, :, 6:7], wts[:, :, 7:8]),
                                                  (tok[:, 0:TT].rearrange("p (t o) -> p t o", o=1), tok[:, TT:2 * TT].rearrange("p (t o) -> p t o", o=1)))):
                    tt(info[:, :, which, :], one, a1.to_broadcast([P, TT, NE]), ALU.mult)
                    tt(rtmp, two_, a2.to_broadcast([P, TT, NE]), ALU.mult)
                    v.drain()
                    tt(info[:, :, which, :], info[:, :, which, :], rtmp, ALU.add)
                    v.drain()
                ts(more[:, 0:7], c(C_THR, 7), cnt_s[:, 0:1], None, ALU.is_lt)
                v.drain()
                v.tensor_reduce(rounds_f[:, 0:1], more[:, 0:7], AX.X, ALU.add)
                v.drain()
                v.tensor_copy(rounds_i[0:1, bass.ds(2 * l, 2)], rounds_f[0:1, :])
                v.drain()
                stt(rounds_f[:, 1:2], rounds_f[:, 0:1], float(PAIRS), rounds_f[:, 1:2], ALU.mult, ALU.add)
                v.drain()
                v.tensor_copy(rounds_i[0:1, bass.ds(2 * l + 3, 1)], rounds_f[0:1, 1:2]).then_inc(route_ok, 1)
                dve.wait_ge(inf_ok, n0 + 1)
                slots(0).then_inc(ix_ok, 1)
                second_half(n0, 0)
                turned(n0)
                with dve.Fori(0, PAIRS // 2 - 1) as it:
                    pair(it, 0)
                    pair(it, 1)
                pair(PAIRS // 2 - 1, 0, 1)
                pair(PAIRS // 2 - 1, 1, 0)

                def more_experts(r, p, q):
                    with dve.If(p == 0):
                        ts(rankm, rankm, -float(CAP), None, ALU.add)
                        v.drain()
                    need(dve, ysc[0], (l + 1) * (PAIRS // 2) * 16)
                    need(dve, ysc[1], (l + 1) * (PAIRS // 2) * 16)
                    need(dve, ov_sc, q * 16)
                    choose(0, 2 * p, ov_sel)
                    dve.wait_ge(ov_ga, q + 1)
                    v.tensor_copy(xg[:, 0:T], bank[0][:, :])
                    slots(0)
                    v.tensor_copy(xg[:, T:D], bank[1][:, :]).then_inc(ov_xg, 1)
                    dve.wait_ge(ov_xt, q + 1)
                    for kh in range(2):
                        last = v.tensor_copy(xgt[:, 4 * kh:4 * kh + 4, :], bank[2 + kh][:, :].rearrange("p (k n) -> p k n", k=4))
                    last.then_inc(ov_xe, 1)
                    dve.wait_ge(ov_sil, q + 1)
                    tt(z[:, :], bank[4][:, FE:2 * FE], sil[:, :], ALU.mult).then_inc(ov_z, 1)
                    dve.wait_ge(ov_zt, q + 1)
                    v.tensor_copy(zt[:, :, :], bank[5][:, 0:FE].rearrange("p (f n) -> p f n", f=2)).then_inc(ov_ze, 1)
                    dve.wait_ge(ov_dn, q + 1)
                    ts(yb[:, 0, 0:T], bank[6][:, :], wslot[:, 0:1], None, ALU.mult)
                    ts(yb[:, 0, T:D], bank[7][:, :], wslot[:, 0:1], None, ALU.mult).then_inc(ov_y, 1)

                overflow(dve, l, more_experts)

                for t in range(TT):
                    dve.wait_ge(yl_ld[0][t], (l + 1) * 16)
                    tt(x[:, t, :], x[:, t, :], yld[:, 0, t, :], ALU.add)
                    if t:
                        mean(t - 1, (2 * l + 2) * TT + t - 1)
                    v.drain()
                    dve.wait_ge(yl_ld[1][t], (l + 1) * 16)
                    tt(x[:, t, :], x[:, t, :], yld[:, 1, t, :], ALU.add).then_inc(x_ok, 1)
                    if t:
                        rstd(slice(t - 1, t), (2 * l + 2) * TT + t - 1).then_inc(rs_ok, 1)

            def final(t):
                dve.wait_ge(xn_ok, L * TT + t + 1)
                tt(yld[:, 1, t, :], xn[:, t, :], g_row[:, :], ALU.mult).then_inc(fin_ok, 1)

            dve.wait_ge(gr_ld, (L + 1) * 16)
            final(0)
            mean(TT - 1, 2 * L * TT + TT - 1)
            final(1)
            rstd(slice(TT - 1, TT), 2 * L * TT + TT - 1).then_inc(rs_ok, 1)
            final(2)
            final(3)

        @block.gpsimd
        def _(pool):
            g = nc.gpsimd
            pool.wait_ge(x_ld[0], 16)
            for s, a, b in MASK_PARTS:
                pool.dma_start(mask_f32[:, a:b], masks[:, a:b]).then_inc(s, ahead[s])
            pool.sem_inc(mlo_ok, ahead[mlo_ok] + 1)
            with pool.Fori(0, L) as l:
                pool.wait_ge(x_ok, l * TT + 1)
                pool.dma_start(par[:, :], params[bass.ds(l, 1), :, :].rearrange("o p n -> p (o n)")).then_inc(par_ld, 16)
                for i, (b, kind, idx) in enumerate(QKV):
                    if kind == V:
                        continue
                    r = ROPES[i]
                    pool.wait_ge(sw_ld[r % 2], (l * SWAPS[r % 2] + r // 2 + 1) * 64)
                    g.tensor_tensor(swp[:, r % 2, :], swp[:, r % 2, :], c(C_SIN, T), ALU.mult).then_inc(sn_ok, 1)
                    pool.wait_ge(sn_ok, l * ROPES[NQ] + r + 1)
                    pool.wait_ge(pj_dve, l * ROPES[NQ] + r + 1)
                    if b == 0:
                        g.tensor_tensor(qk_a[:, idx, :], rca[:, r % 2, :], swp[:, r % 2, :], ALU.add).then_inc(rope_ok, 1)
                    elif idx == 1:
                        g.tensor_tensor(qk_b[b - 1][:, idx, :], rca[:, r % 2, :], swp[:, r % 2, :], ALU.add).then_inc(rope_ok, 1)
                    else:
                        g.tensor_tensor(in_order(qk_b[b - 1][:, idx, :]), by_residue(rca[:, r % 2, :]), by_residue(swp[:, r % 2, :]),
                                        ALU.add).then_inc(rope_ok, 1)
                with pool.Fori(0, KD // 2) as it:
                    for half in range(2):
                        n = l * KD + it * 2 + half
                        need(pool, br_ok, n + 2)
                        g.tensor_tensor(mab[:, half, 0, :], mab[:, half, 0, :], mab[:, half, 1, :], ALU.add).then_inc(sum_ok, 1)
                        pool.wait_ge(mhi_ok, n + 1)
                        g.tensor_tensor(m_lo[:, bass.ds(it * 2 + half, 1), :].rearrange("p o n -> p (o n)"), mab[:, half, 0, :],
                                        m_hi[:, bass.ds(it * 2 + half, 1), :].bitcast(FP32).rearrange("p o n -> p (o n)"),
                                        ALU.subtract).then_inc(mlo_ok, 1)
                need(pool, mlo_ok, l * KD + KD + 1)
                pool.dma_start(g_row[:, :], g_rows[bass.ds(l, 1), :, :].rearrange("o p n -> p (o n)")).then_inc(gr_ld, 16)

                for t in range(TT):
                    pool.wait_ge(h2hi_ok, l * TT + t + 1)
                    g.tensor_tensor(h2_lo[:, t, :], xn2[:, t % 2, :], h2_hi[:, t, :].bitcast(FP32), ALU.subtract).then_inc(h2lo_ok, 1)

                def scatter(s, done):
                    pool.indirect_dma_start(out=y_rows[:, :], out_offset=bass.IndirectOffsetOnAxis(ap=idx_row[:, s:s + 1].bitcast(U32), axis=0),
                                            in_=yb[:, s, :], in_offset=None, bounds_check=2 * T - 1, oob_is_err=False).then_inc(done, 16)

                with pool.Fori(0, PAIRS // 2) as it:
                    for s in range(2):
                        n = l * PAIRS + it * 2 + s
                        need(pool, ya_ok, n + 1)
                        hold(pool, yd_ok, n + 1 + ahead[yd_ok])
                        scatter(s, ysc[s])

                def more_experts(r, p, q):
                    hold(pool, ov_y, q + 1)
                    scatter(0, ov_sc)

                overflow(pool, l, more_experts)
            pool.wait_ge(x_ok, L * TT + 1)
            pool.dma_start(g_row[:, :], g_rows[L, :, :]).then_inc(gr_ld, 16)


def constants(np):
    inv = (1.0 / (np.float32(10000.0) ** (np.arange(0, DH, 2, dtype=np.float32) / np.float32(DH)))).astype(np.float32)
    ang = (np.arange(T, dtype=np.float32)[:, None] * inv[None, :]).astype(np.float32)
    cos, sin = np.cos(ang).T.astype(np.float32), np.sin(ang).T.astype(np.float32)
    k = np.zeros((P, C_END), np.float32)
    k[:, C_COS:C_COS + T] = np.concatenate([cos] * 4)
    k[:, C_SIN:C_SIN + T] = np.concatenate([-sin, sin] * 2)
    k[:, C_ID:C_ID + P] = np.eye(P)
    k[:, C_TRI:C_TRI + P] = np.triu(np.ones((P, P)), 1)
    k[:, C_ONE:C_ONE + P] = 1.0
    k[:, C_IOTA:C_IOTA + CAP] = np.arange(CAP)
    tok = np.arange(T).reshape(TT, P).T
    k[:, C_TOK:C_TOK + TT] = tok - BIG
    k[:, C_TOK + TT:C_TOK + 2 * TT] = tok + T - BIG
    k[:, C_THR:C_THR + 7] = CAP * np.arange(1, 8)
    q = np.arange(P)[:, None]
    off = -1e30
    ma = np.where(np.abs(np.arange(-P, 2 * P)[None, :] - q) <= 128, 0.0, off)
    place = np.arange(P)
    tokens = 16 * (place % 32) + 4 * (place // 32)
    mb = [np.where(np.abs(np.arange(T)[None, :] - (tokens + r)[:, None]) <= 64, 0.0, off) for r in range(4)]
    m1 = np.where(np.abs(tokens[None, :] // 4 - tokens[:, None] // 4) <= 64, 0.0, off)
    m2 = np.where(tokens[None, :] % 16 == tokens[:, None] % 16, 0.0, off)
    return k, np.concatenate([ma, *mb, m1, m2], axis=1).astype(np.float32)


def lay_out(np, w):
    w_in, L = w["w_in"], w["w_in"].shape[0]
    stream = np.zeros((L, NT, P, KD, P), np.float32)

    def tile(cols):
        return w_in[:, :, cols].reshape(L, KD, P, len(cols)).transpose(0, 2, 1, 3)

    ar = np.arange
    a_q = [np.concatenate([j * DH + ar(DH), (j + 4) * DH + ar(DH)]) for j in range(4)]
    for i, (b, kind, idx) in enumerate(QKV):
        if b == 0:
            cols = 640 + ar(P) if kind == V else 512 + ar(P) if idx == 4 else a_q[idx]
        else:
            pair = (b - 1) * P
            if kind == V:
                cols = 768 + idx * 768 + 512 + pair + ar(P)
            else:
                cols = 768 + (idx // 2) * 768 + (idx % 2) * 256 + pair + ar(P)
        stream[:, i] = tile(cols)
    rows_a = np.concatenate(a_q)
    wa = w["w_branch_a"][:, rows_a, :].reshape(L, 4, P, D)
    wb = w["w_branch_b"].reshape(L, 2, P, D)
    for m in range(KD):
        i = NQ + 3 * m
        cols = m * P + ar(P)
        stream[:, i] = tile(3072 + cols)
        stream[:, i + 1] = tile(4096 + cols)
        stream[:, i + 2, :, 0:4] = wa[..., cols].transpose(0, 2, 1, 3)
        stream[:, i + 2, :, 4:6] = wb[..., cols].transpose(0, 2, 1, 3)
    stream = stream.reshape(L, NT, P, D)
    wo = w["w_out"].reshape(L, 4, 2, P, 2, T)
    for dh in range(2):
        for kp in range(4):
            stream[:, NQ + NGATE + 4 * dh + kp] = wo[:, kp, :, :, dh].transpose(0, 2, 1, 3).reshape(L, P, D)

    def up(a):
        return a.reshape(L, NE, KD, P, FE).transpose(0, 1, 3, 2, 4)

    gu_w = np.concatenate([up(w["w_exp_gate"]), up(w["w_exp_up"])], axis=-1).reshape(L * PAIRS, 2, P, KD * 2 * FE)
    dn_w = w["w_exp_down"].reshape(L, NE, 2, P, D).transpose(0, 1, 3, 2, 4).reshape(L * PAIRS, 2, P, 2 * D)
    router = np.concatenate([w["w_router_group"], w["w_router_expert"]], axis=-1)
    router = router.reshape(L, KD, P, NLOG).transpose(0, 2, 1, 3).reshape(L, P, KD * NLOG)
    bias = np.concatenate([w["b_router_group"], w["b_router_expert"]], axis=-1)
    bias = np.broadcast_to(bias[:, None, :], (L, P, NLOG))
    g_col = w["attn_norm_g"].reshape(L, KD, P).transpose(0, 2, 1)
    order = [h for j in range(4) for h in (j, j + 4)]
    sink = np.broadcast_to(w["a_sink"][:, None, order], (L, P, 8))
    g2_col = w["ffn_norm_g"].reshape(L, KD, P).transpose(0, 2, 1)
    params = np.concatenate([router, bias, g_col, g2_col, sink], axis=-1)
    g_rows = np.concatenate([w["ffn_norm_g"], w["final_norm_g"][None]])
    g_rows = np.broadcast_to(g_rows[:, None, :], (L + 1, P, D))
    return [np.ascontiguousarray(a) for a in (w["x"].reshape(T, D), stream, gu_w, dn_w, params, g_rows)]


def kernel(**inputs):
    import numpy as np
    import concourse.bacc as bacc
    from concourse.bass_utils import run_bass_kernel_spmd

    w = {k: np.asarray(v) for k, v in inputs.items()}
    names = ["x", "stream", "gu_w", "dn_w", "params", "g_rows", "consts", "masks"]
    arrays = dict(zip(names, [*lay_out(np, w), *constants(np)]))
    nc = bacc.Bacc("TRN2", target_bir_lowering=False, num_devices=1)
    args = [nc.dram_tensor(f"in_{n}", arrays[n].shape, FP32, kind="ExternalInput").ap() for n in names]
    args.append(nc.dram_tensor("out_x", (T, D), FP32, kind="ExternalOutput").ap())
    hybrid_encoder(nc, *args)
    r = run_bass_kernel_spmd(nc, [{f"in_{n}": arrays[n] for n in names}], core_ids=[0])
    return r.results[0]["out_x"].reshape(1, T, D)
```
